# Optimizing a Trainium2 kernel written in Bass

```python
import math
import jax, jax.numpy as jnp
from jax import lax
import numpy as np

D_MODEL = 2048
BATCH = 1
SEQ = 256
DEPTH = 1

N_MIXERS = 2
HEAD_DIM = 128
GDN_QK_HEADS = D_MODEL // HEAD_DIM
GDN_V_HEADS = 2 * GDN_QK_HEADS
GDN_CONV = 4
GDN_CHUNK = 64
GDN_DQK = GDN_QK_HEADS * HEAD_DIM
GDN_DV = GDN_V_HEADS * HEAD_DIM
GDN_CONV_CH = 2 * GDN_DQK + GDN_DV
GDN_IN = GDN_CONV_CH + GDN_DV + 2 * GDN_V_HEADS
NSA_Q_HEADS = D_MODEL // HEAD_DIM
NSA_KV_HEADS = NSA_Q_HEADS // 4
NSA_GROUP = NSA_Q_HEADS // NSA_KV_HEADS
N_BRANCH = 3
CMP_LEN = 32
CMP_STRIDE = 16
SLC_LEN = 64
SLC_TOP = 16
WINDOW = 512
NSA_QBLOCK = 64
NSA_DQ = NSA_Q_HEADS * HEAD_DIM
NSA_DKV = NSA_KV_HEADS * HEAD_DIM
NSA_IN = NSA_DQ + 6 * NSA_DKV + NSA_Q_HEADS * N_BRANCH
_FF_RAW = -(-8 * D_MODEL // 3)
D_FF = -(-_FF_RAW // 256) * 256
ROPE_THETA = 10000.0
POS_OFFSET_MAX = 32768
LN_EPS = 1e-5
NORM_EPS = 1e-6
ALPHA_DN = (2 * DEPTH) ** 0.25
BETA_DN = (8 * DEPTH) ** -0.25


def layer_norm(x, g, b):
    xf = x.astype(jnp.float32)
    mu = jnp.mean(xf, -1, keepdims=True)
    var = jnp.mean(jnp.square(xf - mu), -1, keepdims=True)
    return ((xf - mu) * lax.rsqrt(var + LN_EPS)).astype(x.dtype) * g + b

def l2norm(t):
    tf = t.astype(jnp.float32)
    return tf * lax.rsqrt(jnp.sum(tf * tf, -1, keepdims=True) + NORM_EPS)

def rope_tables(positions):
    inv = ROPE_THETA ** (-jnp.arange(0, HEAD_DIM, 2, dtype=jnp.float32) / HEAD_DIM)
    ang = positions.astype(jnp.float32)[..., None] * inv
    return jnp.cos(ang)[:, :, None, :], jnp.sin(ang)[:, :, None, :]

def apply_rope(t, cos, sin):
    t1, t2 = jnp.split(t.astype(jnp.float32), 2, axis=-1)
    return jnp.concatenate([t1 * cos - t2 * sin, t2 * cos + t1 * sin], -1).astype(t.dtype)

def masked_softmax(s, mask):
    s = jnp.where(mask, s.astype(jnp.float32), -jnp.inf)
    m = jnp.max(s, -1, keepdims=True)
    m = jnp.where(jnp.isfinite(m), m, 0.0)
    p = jnp.exp(s - m)
    den = jnp.sum(p, -1, keepdims=True)
    return p / jnp.where(den > 0, den, 1.0)

def causal_depthwise_conv(t, w):
    return lax.conv_general_dilated(t, w[:, None, :].astype(t.dtype), window_strides=(1,),
                                    padding=[(GDN_CONV - 1, 0)],
                                    dimension_numbers=('NWC', 'WIO', 'NWC'),
                                    feature_group_count=t.shape[-1])

def gated_delta_rule(q, k, v, g, beta):
    B, S, H, dk = k.shape
    dv = v.shape[-1]
    C = GDN_CHUNK
    N = S // C

    def chunks(t):
        return jnp.moveaxis(t.astype(jnp.float32).reshape(B, N, C, H, *t.shape[3:]), 3, 1)

    q, k, v, g, beta = [chunks(t) for t in (q, k, v, g, beta)]
    gc = jnp.cumsum(g, -1)
    idx = jnp.arange(C)
    lower = idx[:, None] >= idx[None, :]
    strict = idx[:, None] > idx[None, :]
    diff = gc[..., :, None] - gc[..., None, :]
    decay = jnp.where(lower, jnp.exp(jnp.where(lower, diff, 0.0)), 0.0)
    kb = k * beta[..., None]
    L = jnp.where(strict, jnp.einsum('bhnid,bhnjd->bhnij', kb, k) * decay, 0.0)
    rhs = jnp.concatenate([v * beta[..., None], kb * jnp.exp(gc)[..., None]], -1)
    sol = lax.linalg.triangular_solve(L + jnp.eye(C, dtype=L.dtype), rhs, left_side=True,
                                      lower=True, unit_diagonal=True)
    u, w = sol[..., :dv], sol[..., dv:]
    a_qk = jnp.where(lower, jnp.einsum('bhnid,bhnjd->bhnij', q, k) * decay, 0.0)
    q_g = q * jnp.exp(gc)[..., None]
    g_last = gc[..., -1]
    k_g = k * jnp.exp(g_last[..., None] - gc)[..., None]
    xs = [jnp.moveaxis(t, 2, 0) for t in (q_g, k_g, u, w, a_qk, g_last)]

    def step(state, inp):
        qg, kg, uu, ww, aa, gl = inp
        v_new = uu - jnp.einsum('bhck,bhkv->bhcv', ww, state)
        o = jnp.einsum('bhck,bhkv->bhcv', qg, state) + jnp.einsum('bhij,bhjv->bhiv', aa, v_new)
        state = state * jnp.exp(gl)[..., None, None] + jnp.einsum('bhck,bhcv->bhkv', kg, v_new)
        return state, o

    state0 = jnp.zeros((B, H, dk, dv), jnp.float32)
    _, o = lax.scan(step, state0, xs)
    return jnp.transpose(o, (1, 0, 3, 2, 4)).reshape(B, S, H, dv)

def gated_deltanet(h, w_in, conv_w, a_log, dt_bias, norm_w, w_out):
    B, S, _ = h.shape
    proj = h @ w_in
    qkv, z, b, a = jnp.split(proj, [GDN_CONV_CH, GDN_CONV_CH + GDN_DV,
                                    GDN_CONV_CH + GDN_DV + GDN_V_HEADS], axis=-1)
    qkv = jax.nn.silu(causal_depthwise_conv(qkv, conv_w))
    q, k, v = jnp.split(qkv, [GDN_DQK, 2 * GDN_DQK], axis=-1)
    rep = GDN_V_HEADS // GDN_QK_HEADS
    q = jnp.repeat(l2norm(q.reshape(B, S, GDN_QK_HEADS, HEAD_DIM)) * HEAD_DIM ** -0.5, rep, axis=2)
    k = jnp.repeat(l2norm(k.reshape(B, S, GDN_QK_HEADS, HEAD_DIM)), rep, axis=2)
    v = v.reshape(B, S, GDN_V_HEADS, HEAD_DIM)
    beta = jax.nn.sigmoid(b.astype(jnp.float32))
    g = -jnp.exp(a_log.astype(jnp.float32)) * jax.nn.softplus(a.astype(jnp.float32) + dt_bias.astype(jnp.float32))
    o = gated_delta_rule(q, k, v, g, beta)
    o = o * lax.rsqrt(jnp.mean(o * o, -1, keepdims=True) + NORM_EPS)
    o = (o.astype(h.dtype) * norm_w) * jax.nn.silu(z.reshape(B, S, GDN_V_HEADS, HEAD_DIM))
    return o.reshape(B, S, GDN_DV) @ w_out

def nsa_attention(h, cos, sin, w_in, cmp_pe, cmp_w1, cmp_w2, w_out):
    B, S, _ = h.shape
    Hq, Hk, G, dh, QB = NSA_Q_HEADS, NSA_KV_HEADS, NSA_GROUP, HEAD_DIM, NSA_QBLOCK
    proj = h @ w_in
    q, kc, vc, ks, vs, kw, vw, gates = jnp.split(proj, [NSA_DQ + i * NSA_DKV for i in range(7)], axis=-1)
    q = apply_rope(q.reshape(B, S, Hq, dh), cos, sin).reshape(B, S, Hk, G, dh) * dh ** -0.5
    kc, ks, kw = [apply_rope(t.reshape(B, S, Hk, dh), cos, sin) for t in (kc, ks, kw)]
    vc, vs, vw = [t.reshape(B, S, Hk, dh) for t in (vc, vs, vw)]
    gates = jax.nn.sigmoid(gates.astype(jnp.float32)).reshape(B, S, Hk, G, N_BRANCH).astype(h.dtype)

    n_cmp = (S - CMP_LEN) // CMP_STRIDE + 1
    c_start = CMP_STRIDE * jnp.arange(n_cmp)
    cmp_idx = c_start[:, None] + jnp.arange(CMP_LEN)[None, :]
    cmp_end = c_start + CMP_LEN - 1

    def compress(t, pe, w1, w2):
        blk = t[:, cmp_idx] + pe[:, None, :]
        blk = jnp.moveaxis(blk, 3, 2).reshape(B, n_cmp, Hk, CMP_LEN * dh)
        return jax.nn.silu(blk @ w1) @ w2

    kcmp = compress(kc, cmp_pe[0], cmp_w1[0], cmp_w2[0])
    vcmp = compress(vc, cmp_pe[1], cmp_w1[1], cmp_w2[1])

    n_slc = S // SLC_LEN
    n_sel = min(SLC_TOP, n_slc)
    ks_blk = jnp.moveaxis(ks.reshape(B, n_slc, SLC_LEN, Hk, dh), 3, 1)
    vs_blk = jnp.moveaxis(vs.reshape(B, n_slc, SLC_LEN, Hk, dh), 3, 1)
    s_start = SLC_LEN * jnp.arange(n_slc)
    overlap = jnp.clip(jnp.minimum(c_start[:, None] + CMP_LEN, s_start[None, :] + SLC_LEN)
                       - jnp.maximum(c_start[:, None], s_start[None, :]), 0, None).astype(jnp.float32) / CMP_LEN
    b_ix = jnp.arange(B)[:, None, None, None]
    h_ix = jnp.arange(Hk)[None, None, :, None]

    kw_pad = jnp.pad(kw, ((0, 0), (WINDOW, 0), (0, 0), (0, 0)))
    vw_pad = jnp.pad(vw, ((0, 0), (WINDOW, 0), (0, 0), (0, 0)))

    def block(i):
        t0 = i * QB
        tpos = t0 + jnp.arange(QB)
        qb = lax.dynamic_slice_in_dim(q, t0, QB, 1)
        gb = lax.dynamic_slice_in_dim(gates, t0, QB, 1)
        s_c = jnp.einsum('bqhgd,bnhd->bqhgn', qb, kcmp)
        p_c = masked_softmax(s_c, (cmp_end[None, :] <= tpos[:, None])[None, :, None, None, :])
        o_c = jnp.einsum('bqhgn,bnhd->bqhgd', p_c.astype(vcmp.dtype), vcmp)
        imp = jnp.einsum('bqhgn,nj->bqhj', p_c, overlap)
        cur = (tpos // SLC_LEN)[None, :, None, None]
        j = jnp.arange(n_slc)
        forced = (j == 0) | (j == cur) | (j == cur - 1)
        imp = jnp.where(j <= cur, jnp.where(forced, jnp.inf, imp), -jnp.inf)
        _, sel = lax.top_k(imp, n_sel)
        k_sel = ks_blk[b_ix, h_ix, sel].reshape(B, QB, Hk, n_sel * SLC_LEN, dh)
        v_sel = vs_blk[b_ix, h_ix, sel].reshape(B, QB, Hk, n_sel * SLC_LEN, dh)
        key_pos = sel[..., None] * SLC_LEN + jnp.arange(SLC_LEN)
        m_s = (sel <= cur)[..., None] & (key_pos <= tpos[None, :, None, None, None])
        s_s = jnp.einsum('bqhgd,bqhmd->bqhgm', qb, k_sel)
        p_s = masked_softmax(s_s, m_s.reshape(B, QB, Hk, 1, n_sel * SLC_LEN))
        o_s = jnp.einsum('bqhgm,bqhmd->bqhgd', p_s.astype(v_sel.dtype), v_sel)
        kwb = lax.dynamic_slice_in_dim(kw_pad, t0, WINDOW + QB, 1)
        vwb = lax.dynamic_slice_in_dim(vw_pad, t0, WINDOW + QB, 1)
        kpos = t0 - WINDOW + jnp.arange(WINDOW + QB)
        m_w = (kpos[None, :] <= tpos[:, None]) & (kpos[None, :] > tpos[:, None] - WINDOW) & (kpos[None, :] >= 0)
        s_w = jnp.einsum('bqhgd,bkhd->bqhgk', qb, kwb)
        p_w = masked_softmax(s_w, m_w[None, :, None, None, :])
        o_w = jnp.einsum('bqhgk,bkhd->bqhgd', p_w.astype(vwb.dtype), vwb)
        return gb[..., 0:1] * o_c + gb[..., 1:2] * o_s + gb[..., 2:3] * o_w

    o = lax.map(block, jnp.arange(S // QB))
    o = jnp.moveaxis(o, 0, 1).reshape(B, S, NSA_DQ)
    return o @ w_out

def swiglu(h, w_gu, w_down):
    gate, up = jnp.split(h @ w_gu, 2, axis=-1)
    return (jax.nn.silu(gate) * up) @ w_down

def first_inputs(seed: int = 0) -> dict:
    key = jax.random.key(seed)
    k = jax.random.split(key, 24)
    n_gdn = (DEPTH + N_MIXERS - 1) // N_MIXERS
    n_nsa = DEPTH // N_MIXERS

    def w(kk, shape, fan_in, gain=1.0):
        return jax.random.normal(kk, shape, jnp.float32) * (gain * fan_in ** -0.5)

    x = jax.random.normal(k[0], (BATCH, SEQ, D_MODEL), jnp.float32)
    c = jax.random.normal(k[1], (BATCH, D_MODEL), jnp.float32)
    start = jax.random.randint(k[2], (BATCH, 1), 0, POS_OFFSET_MAX, dtype=jnp.int32)
    positions = start + jnp.arange(SEQ, dtype=jnp.int32)[None, :]
    mod_w = w(k[3], (DEPTH, D_MODEL, 6 * D_MODEL), D_MODEL, 0.2)
    mod_b = 0.01 * jax.random.normal(k[4], (DEPTH, 6 * D_MODEL), jnp.float32)
    ln_g = 1.0 + 0.05 * jax.random.normal(k[5], (DEPTH, 2, D_MODEL), jnp.float32)
    ln_b = 0.01 * jax.random.normal(k[6], (DEPTH, 2, D_MODEL), jnp.float32)
    ffn_w_gu = w(k[7], (DEPTH, D_MODEL, 2 * D_FF), D_MODEL)
    ffn_w_down = w(k[8], (DEPTH, D_FF, D_MODEL), D_FF, BETA_DN)
    gdn_w_in = w(k[9], (n_gdn, D_MODEL, GDN_IN), D_MODEL)
    gdn_conv_w = w(k[10], (n_gdn, GDN_CONV, GDN_CONV_CH), GDN_CONV)
    gdn_a_log = jnp.log(jax.random.uniform(k[11], (n_gdn, GDN_V_HEADS), jnp.float32, 1.0, 16.0))
    dt = jnp.exp(jax.random.uniform(k[12], (n_gdn, GDN_V_HEADS), jnp.float32, math.log(1e-3), math.log(1e-1)))
    gdn_dt_bias = dt + jnp.log(-jnp.expm1(-dt))
    gdn_norm_w = 1.0 + 0.05 * jax.random.normal(k[13], (n_gdn, HEAD_DIM), jnp.float32)
    gdn_w_out = w(k[14], (n_gdn, GDN_DV, D_MODEL), GDN_DV, BETA_DN)
    nsa_w_in = w(k[15], (n_nsa, D_MODEL, NSA_IN), D_MODEL)
    nsa_cmp_pe = 0.1 * jax.random.normal(k[16], (n_nsa, 2, CMP_LEN, HEAD_DIM), jnp.float32)
    nsa_cmp_w1 = w(k[17], (n_nsa, 2, CMP_LEN * HEAD_DIM, HEAD_DIM), CMP_LEN * HEAD_DIM)
    nsa_cmp_w2 = w(k[18], (n_nsa, 2, HEAD_DIM, HEAD_DIM), HEAD_DIM)
    nsa_w_out = w(k[19], (n_nsa, NSA_DQ, D_MODEL), NSA_DQ, BETA_DN)
    return {'x': x, 'c': c, 'positions': positions, 'mod_w': mod_w, 'mod_b': mod_b,
            'ln_g': ln_g, 'ln_b': ln_b, 'ffn_w_gu': ffn_w_gu, 'ffn_w_down': ffn_w_down,
            'gdn_w_in': gdn_w_in, 'gdn_conv_w': gdn_conv_w, 'gdn_a_log': gdn_a_log,
            'gdn_dt_bias': gdn_dt_bias, 'gdn_norm_w': gdn_norm_w, 'gdn_w_out': gdn_w_out,
            'nsa_w_in': nsa_w_in, 'nsa_cmp_pe': nsa_cmp_pe, 'nsa_cmp_w1': nsa_cmp_w1,
            'nsa_cmp_w2': nsa_cmp_w2, 'nsa_w_out': nsa_w_out}

def first_block(x, c, positions, mod_w, mod_b, ln_g, ln_b, ffn_w_gu, ffn_w_down,
              gdn_w_in, gdn_conv_w, gdn_a_log, gdn_dt_bias, gdn_norm_w, gdn_w_out,
              nsa_w_in, nsa_cmp_pe, nsa_cmp_w1, nsa_cmp_w2, nsa_w_out):
    cos, sin = rope_tables(positions)
    cond = jax.nn.silu(c)
    for i in range(DEPTH):
        mod = (cond @ mod_w[i] + mod_b[i])[:, None, :]
        sh1, sc1, ga1, sh2, sc2, ga2 = jnp.split(mod, 6, axis=-1)
        j = i // N_MIXERS
        h = x * (1 + sc1) + sh1
        if i % N_MIXERS == 0:
            y = gated_deltanet(h, gdn_w_in[j], gdn_conv_w[j], gdn_a_log[j], gdn_dt_bias[j],
                               gdn_norm_w[j], gdn_w_out[j])
        else:
            y = nsa_attention(h, cos, sin, nsa_w_in[j], nsa_cmp_pe[j], nsa_cmp_w1[j],
                              nsa_cmp_w2[j], nsa_w_out[j])
        x = layer_norm(ALPHA_DN * x + (1 + ga1) * y, ln_g[i, 0], ln_b[i, 0])
        h = x * (1 + sc2) + sh2
        y = swiglu(h, ffn_w_gu[i], ffn_w_down[i])
        x = layer_norm(ALPHA_DN * x + (1 + ga2) * y, ln_g[i, 1], ln_b[i, 1])
    return x


CHUNK = 64

CONV_WIDTH = D_MODEL
CONV_K = 3
SSM_WIDTH = D_MODEL // 2
SSM_GROUP = 16
SSM_GROUPS = SSM_WIDTH // SSM_GROUP
SSM_STATE = 64
DT_MIN = 0.001
DT_MAX = 0.1
RMS_EPS = 1e-6

_SIZES = (CONV_WIDTH, CONV_WIDTH, CONV_WIDTH, CONV_WIDTH,
          SSM_WIDTH, SSM_WIDTH,
          D_MODEL, D_MODEL)
N_IN = int(sum(_SIZES))
SPLITS = tuple(int(s) for s in np.cumsum(_SIZES)[:-1])


def rmsnorm(x, g):
    x32 = x.astype(jnp.float32)
    y = x32 * lax.rsqrt(jnp.mean(x32 * x32, axis=-1, keepdims=True) + RMS_EPS)
    return (y * g.astype(jnp.float32)).astype(x.dtype)

def causal_depthwise_conv_2(v, w):
    L = v.shape[1]
    vp = jnp.pad(v, ((0, 0), (CONV_K - 1, 0), (0, 0)))
    out = w[0] * vp[:, 0:L]
    for k in range(1, CONV_K):
        out = out + w[k] * vp[:, k:k + L]
    return out

def s5_scan(u, a_re, a_im, log_dt, b_re, b_im, c_re, c_im, d_skip):
    bsz, L, _ = u.shape
    f32 = jnp.float32
    ug = u.astype(f32).reshape(bsz, L, SSM_GROUPS, SSM_GROUP)
    lam = lax.complex(a_re.astype(f32), a_im.astype(f32))
    dt = jnp.exp(log_dt.astype(f32))[:, None]
    lam_bar = jnp.exp(lam * dt)
    b = lax.complex(b_re.astype(f32), b_im.astype(f32))
    b_bar = ((lam_bar - 1.0) / lam)[..., None] * b
    bu = jnp.einsum('gpc,blgc->blgp', b_bar, ug.astype(jnp.complex64))
    a = jnp.broadcast_to(lam_bar, bu.shape)

    def combine(e1, e2):
        a1, h1 = e1
        a2, h2 = e2
        return a1 * a2, a2 * h1 + h2

    _, h = lax.associative_scan(combine, (a, bu), axis=1)
    c = lax.complex(c_re.astype(f32), c_im.astype(f32))
    y = jnp.einsum('gcp,blgp->blgc', c, h).real + d_skip.astype(f32) * ug
    return y.reshape(bsz, L, SSM_WIDTH)

def hybrid_layer(x, norm_g, w_in, conv_w, w_out_a, a_re, a_im, log_dt, b_re, b_im,
                 c_re, c_im, d_skip, w_glu, b_glu, w_out_b, w_o):
    h = rmsnorm(x, norm_g)
    proj = jnp.einsum('bld,dn->bln', h, w_in)
    v, bg, cg, za, u, zb, ga, gb = jnp.split(proj, SPLITS, axis=-1)
    ya = bg * causal_depthwise_conv_2(cg * v, conv_w)
    ya = jnp.einsum('blc,cd->bld', ya * jax.nn.silu(za), w_out_a)
    yb = jax.nn.gelu(s5_scan(u, a_re, a_im, log_dt, b_re, b_im, c_re, c_im, d_skip))
    yb = yb * jax.nn.sigmoid(jnp.einsum('blc,ce->ble', yb, w_glu.astype(jnp.float32))
                             + b_glu.astype(jnp.float32))
    yb = yb.astype(x.dtype)
    yb = jnp.einsum('blc,cd->bld', yb * jax.nn.silu(zb), w_out_b)
    m = jax.nn.sigmoid(ga) * ya + jax.nn.sigmoid(gb) * yb
    return x + jnp.einsum('bld,de->ble', m, w_o)

def second_inputs(seed: int = 0) -> dict:
    key = jax.random.key(seed)
    ks = jax.random.split(key, 20)
    f32 = jnp.float32
    n = lambda k, shape, s: jax.random.normal(k, shape, f32) * s
    res_scale = 1.0 / math.sqrt(2.0 * DEPTH)
    G, P, c = SSM_GROUPS, SSM_STATE, SSM_GROUP
    a_im_base = math.pi * jnp.arange(P, dtype=f32)
    return {
        "x": n(ks[0], (BATCH, SEQ, D_MODEL), 1.0),
        "norm_g": 1.0 + n(ks[1], (DEPTH, D_MODEL), 0.02),
        "w_in": n(ks[2], (DEPTH, D_MODEL, N_IN), D_MODEL ** -0.5),
        "conv_w": n(ks[3], (DEPTH, CONV_K, CONV_WIDTH), CONV_K ** -0.5),
        "w_out_a": n(ks[4], (DEPTH, CONV_WIDTH, D_MODEL), CONV_WIDTH ** -0.5),
        "a_re": -0.5 + n(ks[5], (DEPTH, G, P), 0.01),
        "a_im": a_im_base + n(ks[6], (DEPTH, G, P), 0.01),
        "log_dt": jax.random.uniform(ks[7], (DEPTH, G), f32,
                                     math.log(DT_MIN), math.log(DT_MAX)),
        "b_re": n(ks[8], (DEPTH, G, P, c), (2.0 * c) ** -0.5),
        "b_im": n(ks[9], (DEPTH, G, P, c), (2.0 * c) ** -0.5),
        "c_re": n(ks[10], (DEPTH, G, c, P), (2.0 * P) ** -0.5),
        "c_im": n(ks[11], (DEPTH, G, c, P), (2.0 * P) ** -0.5),
        "d_skip": n(ks[12], (DEPTH, G, c), 1.0),
        "w_glu": n(ks[13], (DEPTH, SSM_WIDTH, SSM_WIDTH), SSM_WIDTH ** -0.5),
        "b_glu": n(ks[14], (DEPTH, SSM_WIDTH), 0.02),
        "w_out_b": n(ks[15], (DEPTH, SSM_WIDTH, D_MODEL), SSM_WIDTH ** -0.5),
        "w_o": n(ks[16], (DEPTH, D_MODEL, D_MODEL), D_MODEL ** -0.5 * res_scale),
        "final_g": 1.0 + n(ks[17], (D_MODEL,), 0.02),
    }

def second_block(x, norm_g, w_in, conv_w, w_out_a, a_re, a_im, log_dt, b_re, b_im,
              c_re, c_im, d_skip, w_glu, b_glu, w_out_b, w_o, final_g):
    for i in range(DEPTH):
        x = hybrid_layer(x, norm_g[i], w_in[i], conv_w[i], w_out_a[i], a_re[i], a_im[i],
                         log_dt[i], b_re[i], b_im[i], c_re[i], c_im[i], d_skip[i],
                         w_glu[i], b_glu[i], w_out_b[i], w_o[i])
    return rmsnorm(x, final_g)


def setup_inputs(seed=0):
    out = dict(first_inputs(seed))
    for name, value in second_inputs(seed + 1).items():
        if name != "x":
            out[name + "_2"] = value
    return out


def reference(
    x, c, positions, mod_w, mod_b, ln_g, ln_b, ffn_w_gu, ffn_w_down, gdn_w_in, gdn_conv_w,
    gdn_a_log, gdn_dt_bias, gdn_norm_w, gdn_w_out, nsa_w_in, nsa_cmp_pe, nsa_cmp_w1, nsa_cmp_w2,
    nsa_w_out, norm_g_2, w_in_2, conv_w_2, w_out_a_2, a_re_2, a_im_2, log_dt_2, b_re_2, b_im_2,
    c_re_2, c_im_2, d_skip_2, w_glu_2, b_glu_2, w_out_b_2, w_o_2, final_g_2,
):
    x = first_block(
        x, c, positions, mod_w, mod_b, ln_g, ln_b, ffn_w_gu, ffn_w_down, gdn_w_in, gdn_conv_w,
        gdn_a_log, gdn_dt_bias, gdn_norm_w, gdn_w_out, nsa_w_in, nsa_cmp_pe, nsa_cmp_w1,
        nsa_cmp_w2, nsa_w_out,
    )
    return second_block(
        x, norm_g_2, w_in_2, conv_w_2, w_out_a_2, a_re_2, a_im_2, log_dt_2, b_re_2, b_im_2,
        c_re_2, c_im_2, d_skip_2, w_glu_2, b_glu_2, w_out_b_2, w_o_2, final_g_2,
    )


_drawn_inputs = setup_inputs


def setup_inputs(seed=0):
    import zlib

    import numpy as np

    out = dict(_drawn_inputs(seed))
    spreads = {}
    factors = {'mod_b': 4.884,
     'ln_b': 3.617,
     'gdn_norm_w': 3.353,
     'norm_g_2': 5.887,
     'a_re_2': 64.0,
     'a_im_2': 64.0,
     'log_dt_2': 64.0,
     'b_re_2': 64.0,
     'b_im_2': 64.0,
     'c_re_2': 64.0,
     'c_im_2': 64.0,
     'b_glu_2': 200.0,
     'final_g_2': 22.039,
     'd_skip_2': 4.817,
     'w_glu_2': 7.005,
     'w_out_b_2': 4.262}
    for name, (base, spread) in spreads.items():
        noise = np.random.default_rng([zlib.crc32(name.encode()), seed]).standard_normal(out[name].shape)
        drawn = base * np.exp(spread * noise) if base else spread * noise
        out[name] = __import__('jax').numpy.asarray(drawn.astype(out[name].dtype))
    for name, factor in factors.items():
        out[name] = (out[name] * factor).astype(out[name].dtype)
    return out
```

```python
import math
from contextlib import ExitStack

import concourse.bass as bass
import concourse.mybir as mybir

F32 = mybir.dt.float32
ALU = mybir.AluOpType
ACT = mybir.ActivationFunctionType
AX = mybir.AxisListType

P = 128
T = 256
TT = T // P
D = 2048
KD = D // P
NH = 32
NQK = 16
NIT = NQK // 2
VH = 4
GDN_IN = 12352
GQ, GK, GV, GZ, GB, GA = 0, 2048, 4096, 8192, 12288, 12320
FF = 5632
KF = FF // P
N2 = 14336
SSMW = 1024
PAIRS = 32
ALPHA = 2.0 ** 0.25
LN_EPS = 1e-5
EPS = 1e-6
LEVELS = (2, 4, 8, 16, 32)
BIG = -1.0e30

V_MODB, V_C, V_FG = 0, 96, 112
V_LNG, V_LNB, V_NG, V_CW2 = 128, 160, 192, 208
V_CW = 256
V_NW, V_BGLU, V_DSK = 512, 513, 521
V_ROWS = (128, 128, 128, 128, 17)

PE_STEPS = ("norms+rows", "vtok", "gram", "t2", "x2", "tx2", "u2+x4", "tx4", "u4+x8", "tx8",
            "u8+x16", "tx16", "u16+x32", "tx32", "u32+x64", "ux64", "v0", "s+o0", "r+qs", "v1",
            "o1", "otr", "mod")


def order(*names):
    return {n: i + 1 for i, n in enumerate(names)}


PEO = order("ssq", "rows", "vtok", "gram", "ktok", "t2", "x2", "tx2", "u2", "x4", "tx4", "u4", "x8",
            "tx8", "u8", "x16", "tx16", "u16", "x32", "tx32", "u32", "x64", "ux64", "v0", "s", "o0", "r",
            "qs", "v1", "o1", "otr", "mod")
VO = order("scal", "qkn", "dt", "lt", "at", "u2", *[f"{a}{s}" for s in LEVELS for a in ("x", "t")],
           "x64", "u64", "o0", "rhs1", "o1", "on", "og", "modt")
AO = order("rn", "exp", "vtok", "kg", "t2", *[f"u{s}" for s in LEVELS], "v0", "s", "qs", "v1",
           "rstd", "qkv", "z")
GO = order("sq", "rowm")


LN_QSCALE = -0.5 * math.log(128.0)
N_VEC = 12
U_OUT = 12 * NIT
U_FF = U_OUT + 32
U_DOWN = U_FF + 8 * (KF // 4)
U_HYB = U_DOWN + KF
W_GDN = 64 * NIT
G_DOWN = 4


def first_of(*runs):
    at, n = {}, 0
    for name, count in runs:
        at[name] = n + 1
        n += count
    return at


AN = first_of(("sqa", 4), ("rsa", 1), ("x1_", 4), ("sqb", 4), ("rsb", 1), ("x2_", 4), ("sqc", 4), ("rsc", 1),
              ("sqd", 4), ("rsd", 1))
AN["x1"], AN["x2"] = AN["x1_"] + 3, AN["x2_"] + 3
VN = first_of(("da", 4), ("ha", 4), ("db", 4), ("nb", 4), ("hc", 4), ("xo", 4))
U_MIX = U_HYB + 16
U_GATE = U_MIX + 64
U_GLU = U_GATE + 32
U_OA = U_GLU + 4
U_OB = U_OA + 16
U_O = U_OB + 8
C_V, C_BG, C_CG, C_ZA, C_U, C_ZB, C_GA, C_GB = 0, 2048, 4096, 6144, 8192, 9216, 10240, 12288
N_RAW = 3 + 2 * 2 * 5
MAGIC = 12582912.0
LN2_HI = 0.693359375
LN2_LO = math.log(2.0) - LN2_HI
TURN = (6.28125, 0.0019350051879882812, 2 * math.pi - 6.28125 - 0.0019350051879882812)
AO0 = 2
N_CST = 2 + 4 + 1 + 1 + 7
A0 = {"vec": 2, "cond": 3, "x3": 7, "beta": 8, "sp": 10, "tok": 13}
V0 = {"h": 1, "cw": 2, "gc": 3, "tok": 4}


def build(nc, A, out, stop=None):
    ctx = ExitStack()
    with ctx:
        def sb(name, shape, dt=F32):
            return ctx.enter_context(nc.sbuf_tensor(name, shape, dt))

        def sem(name):
            return ctx.enter_context(nc.semaphore(name))

        ident = sb("ident", [P, P])
        ones = sb("ones", [P, P])
        onesd = sb("onesd", [P, P])
        mneg = sb("mneg", [P, P])
        m1t = sb("m1t", [P, P])
        masks = sb("masks", [P, 6, P])
        msk = {s: masks[:, i, :] for i, s in enumerate(LEVELS + (64,))}
        vc = sb("vc", [P, 640])
        modt = sb("modt", [P, 96])
        cst = sb("cst", [P, 4])
        sc1p = sb("sc1p", [P, KD])
        condt = sb("condt", [P, KD])
        xT = sb("xT", [P, KD, T])
        hT = sb("hT", [P, KD, T])
        wr = [sb(f"wr{i}", [P, 4, 512]) for i in range(4)]
        ARENA = 34300
        arena = sb("arena", [P, ARENA])
        at = [0]

        def take(*shape):
            n = 1
            for s in shape:
                n *= s
            v = arena[:, at[0]:at[0] + n]
            at[0] += n
            assert at[0] <= ARENA, at
            names = "abcd"[:len(shape)]
            return v.rearrange(f"p ({' '.join(names)}) -> p {' '.join(names)}",
                               **{k: s for k, s in zip(names[:-1], shape[:-1])}) if len(shape) > 1 else v

        oT = take(NH, T)
        xtok = oT[:, 0:16, :].rearrange("p a b -> p (a b)").rearrange("p (t n) -> p t n", t=TT)
        vstage = oT[:, 16:19, :].rearrange("p a b -> p (a b)")[:, 0:640].rearrange("p (t n) -> p t n", t=5)
        mw = [take(4, 512) for _ in range(2)]
        acc = take(2, 512)
        pend = take(8, T)
        zpend = take(VH, T)
        qk = take(4, T)
        vT = take(VH, T)
        zT = take(VH, T)
        Xb = take(8, P)
        Tb = take(8, P)
        Ub = take(8, P)
        sqb = Xb.rearrange("p a b -> p (a b)")
        rnb = Tb.rearrange("p a b -> p (a b)")
        dTb = take(8, P)
        lTb = take(8, P)
        aTb = take(8, P)
        vtok = take(8, P)
        kg0 = take(VH, P)
        vn0 = take(VH, P)
        vn1 = take(VH, P)
        Sb = take(VH, P)
        rhs1 = take(VH, P)
        ob = take(8, P)
        rowm = take(2, VH, P)
        tk = take(7, NH)
        tkc = take(7, VH)
        cwc = take(4, 8)
        ssq = take(8)
        rstd = take(8)
        bT = take(T)
        aT = take(T)
        wba = lTb.rearrange("p a b -> p (a b)").rearrange("p (k n) -> p k n", k=KD)
        gx = take(4, T)
        alog = take(4)

        at[0] = NH * T
        sqn = take(KD, T)
        rs = take(T)
        hg = take(KF, T)
        sg = take(4, T)
        cols = take(7, KD)
        ga1p, sc2p, g1, b1, ag, ab, ga2p = (cols[:, i, :] for i in range(7))
        BC = take(8, 4, P)
        E1r, E1i, E16r, E16i = (take(PAIRS, 16) for _ in range(4))
        rdec = take(PAIRS)
        gst = take(2, T)
        hst = [take(2, T) for _ in range(2)]
        bcur = [take(4, P) for _ in range(2)]
        ucur = [take(T) for _ in range(2)]
        ptmp = masks[:, 0:4, :].rearrange("p a b -> p (a b)").rearrange("p (a b) -> p a b", a=2)
        at[0] = 0
        braw = [take(PAIRS, 32) for _ in range(2)]
        craw = [take(8, P) for _ in range(2)]
        bbar = [take(PAIRS, 32) for _ in range(2)]
        btmp = take(PAIRS, 32)
        araw = take(3, P)
        ldraw = sb("ldraw", [P, 2])
        prm = take(20, PAIRS)
        assert at[0] <= NH * T
        at[0] = 0
        uT = take(8, T)
        zb = take(8, T)
        yb = take(8, T)
        cgb = take(4, T)
        pb = take(4, T)
        assert at[0] == NH * T
        yaT = take(KD, T)
        take(T)
        sga = take(KD, T)
        sgb = take(KD, T)
        cvb = take(4, T)
        szb = take(4, T)
        tabs = [take(2, T) for _ in range(2)]
        p1 = take(2, T)
        p2 = take(2, T)
        glu = BC.rearrange("p a b c -> p (a b c)")[:, 0:8 * T].rearrange("p (a b) -> p a b", a=8)
        mT, yg, sqo, xo = sga, uT, yaT, sgb
        ostage = [a.rearrange("p a b -> p (a b)")[:, 0:D] for a in (uT, zb)]

        pg = [ctx.enter_context(nc.psum_tensor(f"pg{i}", [P, 1024], F32)) for i in range(2)]
        pd = [ctx.enter_context(nc.psum_tensor(f"pd{i}", [P, 1024], F32)) for i in range(2)]

        s_vec = sem("s_vec")
        s_x = sem("s_x")
        s_wba = sem("s_wba")
        s_w = [sem(f"s_w{i}") for i in range(4)]
        s_mw = [sem(f"s_mw{i}") for i in range(2)]
        s_unit = sem("s_unit")
        s_cd = sem("s_cd")
        s_zo = sem("s_zo")
        s_cv = sem("s_cv")
        s_acc = sem("s_acc")
        s_pe = sem("s_pe")
        s_v = sem("s_v")
        s_a = sem("s_a")
        s_g = sem("s_g")
        s_cst = sem("s_cst")
        s_p0 = sem("s_p0")
        s_a0 = sem("s_a0")
        s_v0 = sem("s_v0")
        s_vv, s_aa, s_gg = sem("s_vv"), sem("s_aa"), sem("s_gg")
        s_ev = sem("s_ev")
        s_hg = sem("s_hg")
        s_pn = sem("s_pn")
        s_vn = sem("s_vn")
        s_an = sem("s_an")
        s_sg = sem("s_sg")
        s_raw = sem("s_raw")
        s_pp = sem("s_pp")
        s_ap = sem("s_ap")
        s_vx = sem("s_vx")
        s_vp = sem("s_vp")
        s_uz = sem("s_uz")
        s_cg = sem("s_cg")
        s_vo = sem("s_vo")
        s_tp = sem("s_tp")
        s_cb = sem("s_cb")
        s_bg = sem("s_bg")
        s_za = sem("s_za")
        s_ya = sem("s_ya")
        s_cur = sem("s_cur")
        s_tab = sem("s_tab")
        s_xp = sem("s_xp")
        s_h = sem("s_h")
        s_yp = sem("s_yp")
        s_yt = sem("s_yt")
        s_gate = sem("s_gate")
        s_gel = sem("s_gel")
        s_glu = sem("s_glu")
        s_yg = sem("s_yg")
        s_m = sem("s_m")
        s_m2 = sem("s_m2")
        s_x3 = sem("s_x3")
        s_po = sem("s_po")
        s_ao = sem("s_ao")
        s_out = sem("s_out")

        def chain(eng, own):
            n = [0]

            def link(ins):
                n[0] += 1
                ins.then_inc(own, 1)
                eng.wait_ge(own, n[0])

            def restart():
                eng.sem_clear(own)
                n[0] = 0
            return link, restart

        w_in = A["gdn_w_in"][0].rearrange("(k p) n -> p k n", p=P)
        mod_w = A["mod_w"][0].rearrange("(k p) n -> p k n", p=P)
        w_out = A["gdn_w_out"][0].rearrange("(k p) n -> p k n", p=P)

        w_in2 = A["w_in_2"][0].rearrange("(k p) n -> p k n", p=P)
        w_oa = A["w_out_a_2"][0].rearrange("(k p) n -> p k n", p=P)
        w_ob = A["w_out_b_2"][0].rearrange("(k p) n -> p k n", p=P)
        w_glu = A["w_glu_2"][0].rearrange("(k p) n -> p k n", p=P)
        w_o = A["w_o_2"][0].rearrange("(k p) n -> p k n", p=P)
        w_gu = A["ffn_w_gu"][0].rearrange("(k p) n -> p k n", p=P)
        w_down = A["ffn_w_down"][0]

        block = ctx.enter_context(nc.Block())

        @block.sync
        def _(sp):
            with nc.allow_non_contiguous_dma("small vectors"):
                rows = []

                def vrow(col, src):
                    n = src.shape[0]
                    tile, r = col // P, col % P
                    assert r + n <= P
                    rows.append((vstage[r:r + n, tile, :], src))
                one = lambda a: a.rearrange("(r c) -> r c", c=P)
                vrow(V_MODB, one(A["mod_b"][0]))
                vrow(V_C, one(A["c"][0]))
                vrow(V_FG, one(A["final_g_2"]))
                vrow(V_LNG, A["ln_g"][0].rearrange("a (r c) -> (a r) c", c=P))
                vrow(V_LNB, A["ln_b"][0].rearrange("a (r c) -> (a r) c", c=P))
                vrow(V_NG, one(A["norm_g_2"][0]))
                vrow(V_CW2, A["conv_w_2"][0].rearrange("a (r c) -> (a r) c", c=P))
                cw = A["gdn_conv_w"][0].rearrange("a (r c) -> (a r) c", c=P)
                vrow(V_CW, cw[0:P, :])
                vrow(V_CW + P, cw[P:2 * P, :])
                vrow(V_NW, A["gdn_norm_w"])
                vrow(V_BGLU, one(A["b_glu_2"][0]))
                vrow(V_DSK, A["d_skip_2"][0].rearrange("(r a) c -> r (a c)", r=8))
                assert len(rows) == N_VEC
                for dst, src in rows:
                    sp.dma_start(dst, src).then_inc(s_vec, 16)
                sp.dma_start(xtok, A["x"][0].rearrange("(t p) n -> p t n", p=P)).then_inc(s_x, 16)
                sp.dma_start(wba, w_in[:, :, GB:GB + 64]).then_inc(s_wba, 16)
                sp.dma_start(alog[0:NH, 0:1], A["gdn_a_log"].rearrange("a h -> h a")).then_inc(s_wba, 16)
                sp.dma_start(alog[0:NH, 1:2], A["gdn_dt_bias"].rearrange("a h -> h a")).then_inc(s_wba, 16)

            def batch_loads(g, first=False):
                for t in range(12):
                    if not (first and t < 4):
                        sp.wait_ge(s_unit, g * 12 + (t - 3))
                    slot, ks = t % 4, slice(4 * (t % 4), 4 * (t % 4) + 4)
                    if t < 4:
                        sp.dma_start(wr[slot][:, :, 0:256], w_in[:, ks, bass.ds(g * 256 + GQ, 256)]).then_inc(s_w[slot], 16)
                        sp.dma_start(wr[slot][:, :, 256:512], w_in[:, ks, bass.ds(g * 256 + GK, 256)]).then_inc(s_w[slot], 16)
                    else:
                        col = g * 512 + (GV if t < 8 else GZ)
                        sp.dma_start(wr[slot][:], w_in[:, ks, bass.ds(col, 512)]).then_inc(s_w[slot], 16)

            batch_loads(0, first=True)
            with sp.Fori(0, NIT - 1) as j:
                batch_loads(j + 1)
            if stop == "gdn":
                sp.wait_ge(s_v, NIT * len(VO))
                sp.dma_start(out.rearrange("p (a b) -> p a b", a=32), oT).then_inc(s_out, 16)
                sp.wait_ge(s_out, 16)
                return

            def load(u, slot, src):
                sp.wait_ge(s_unit, u - 3)
                sp.dma_start(wr[slot][:], src).then_inc(s_w[slot], 16)

            def column_block(w, k4, first, j):
                return w[:, 4 * k4:4 * k4 + 4, first:][:, :, bass.ds(j * 512, 512)]

            with sp.Fori(0, 4) as j:
                for t in range(8):
                    load(j * 8 + (U_OUT + t), t % 4, w_out[:, 4 * t:4 * t + 4, bass.ds(j * 512, 512)])
            with sp.Fori(0, KF // 4) as j:
                for t in range(8):
                    load(j * 8 + (U_FF + t), t % 4, column_block(w_gu, t % 4, FF * (t // 4), j))
            with sp.Fori(0, KF // 4) as j:
                for t in range(4):
                    load(j * 4 + (U_DOWN + t), t, w_down[bass.ds(j * 512, 512), t * 512:(t + 1) * 512]
                         .rearrange("(k p) n -> p k n", p=P))
            if stop != "x2":
                with sp.Fori(0, 2) as j:
                    for t in range(8):
                        load(j * 8 + (U_HYB + t), t % 4, column_block(w_in2, t % 4, (C_U, C_ZB)[t // 4], j))
                with sp.Fori(0, 4) as j:
                    for t in range(16):
                        load(j * 16 + (U_MIX + t), t % 4, column_block(w_in2, t % 4, (C_V, C_CG, C_BG, C_ZA)[t // 4], j))
                with sp.Fori(0, 4) as j:
                    for t in range(8):
                        load(j * 8 + (U_GATE + t), t % 4, column_block(w_in2, t % 4, (C_GA, C_GB)[t // 4], j))
                for t in range(4):
                    load(U_GLU + t, t, w_glu[:, 4 * (t % 2):4 * (t % 2) + 4, (t // 2) * 512:(t // 2 + 1) * 512])
                with sp.Fori(0, 4) as j:
                    for t in range(4):
                        load(j * 4 + (U_OA + t), t, w_oa[:, 4 * t:4 * t + 4, bass.ds(j * 512, 512)])
                with sp.Fori(0, 2) as j:
                    for t in range(4):
                        load(j * 4 + (U_OB + t), t, w_ob[:, 4 * (t % 2):4 * (t % 2) + 4, (t // 2) * 512:][:, :, bass.ds(j * 1024, 512)])
                with sp.Fori(0, 4) as j:
                    for t in range(4):
                        load(j * 4 + (U_O + t), t, w_o[:, 4 * t:4 * t + 4, bass.ds(j * 512, 512)])
                for t in range(TT):
                    sp.wait_ge(s_ao, 4 * (t + 1))
                    sp.dma_start(out[0, t * P:(t + 1) * P, :], ostage[t]).then_inc(s_out, 16)
                sp.wait_ge(s_out, 16 * TT)
            if stop in ("x1", "x2"):
                sp.wait_ge(s_an, AN["x1" if stop == "x1" else "x2"])
                sp.dma_start(out.rearrange("p (a b) -> p a b", a=KD), xT[:]).then_inc(s_out, 16)
                sp.wait_ge(s_out, 16)

        @block.gpsimd
        def _(pool):
            link, restart = chain(pool, s_gg)

            def mod_loads(base, t0, n):
                for t in range(t0, t0 + n):
                    if not (isinstance(base, int) and base + t < 2):
                        pool.wait_ge(s_acc, base + (t - 1))
                    k = t % 4
                    pool.dma_start(mw[t % 2], mod_w[:, 4 * k:4 * k + 4, bass.ds(base * 128 + (t // 4) * 512, 512)])\
                        .then_inc(s_mw[t % 2], 16)

            mod_loads(0, 0, 2)
            nc.gpsimd.memset(ones[:], 1.0).then_inc(s_cst, 1)
            nc.gpsimd.memset(onesd[:], 1.0 / D).then_inc(s_cst, 1)
            for c, v in enumerate((EPS, LN_EPS, LN_QSCALE, 1.0)):
                nc.gpsimd.memset(cst[:, c:c + 1], v).then_inc(s_cst, 1)
            link(nc.gpsimd.memset(ident[:], 0.0))
            nc.gpsimd.affine_select(out=ident[:], in_=ident[:], compare_op=ALU.not_equal, fill=1.0, base=0,
                                    pattern=[[-1, P]], channel_multiplier=1).then_inc(s_cst, 1)
            link(nc.gpsimd.memset(mneg[:], 0.0))
            nc.gpsimd.affine_select(out=mneg[:], in_=mneg[:], compare_op=ALU.is_ge, fill=BIG, base=0,
                                    pattern=[[1, P]], channel_multiplier=-1).then_inc(s_cst, 1)
            for s, m in [(1, m1t)] + list(msk.items()):
                link(nc.gpsimd.memset(m[:], 0.0))
                nb = P // (2 * s)
                half = m[:].rearrange("p (b two s) -> p b two s", two=2, s=s)
                v = half[:, :, 1, :] if s == 1 else half[:, :, 0, :]
                lo, hi = (0, 0) if s == 1 else (s, 2 * s - 1)
                link(nc.gpsimd.memset(v, 1.0))
                link(nc.gpsimd.affine_select(out=v, in_=v, compare_op=ALU.is_ge, fill=0.0, base=-lo,
                                             pattern=[[-2 * s, nb], [0, s]], channel_multiplier=1))
                nc.gpsimd.affine_select(out=v, in_=v, compare_op=ALU.is_ge, fill=0.0, base=hi,
                                        pattern=[[2 * s, nb], [0, s]], channel_multiplier=-1).then_inc(s_cst, 1)
            mod_loads(0, 2, 30)

            def batch(it):
                restart()
                pool.wait_ge(s_a, it * len(AO) + 1)
                nc.gpsimd.tensor_tensor(sqb, qk.rearrange("p a b -> p (a b)"), qk.rearrange("p a b -> p (a b)"),
                                        ALU.mult).then_inc(s_g, 1)
                pool.wait_ge(s_v0, V0["tok"])
                rows = gcT[0:NH].rearrange("p (c t) -> p c t", c=TT).unsqueeze(2).broadcast_to([NH, TT, VH, P])
                pick = ident[0:NH, bass.ds(it * VH, VH)].unsqueeze(1).unsqueeze(3).broadcast_to([NH, TT, VH, P])
                nc.gpsimd.tensor_tensor(rowm[0:NH], rows, pick, ALU.mult).then_inc(s_g, 1)
                mod_loads(it * 8 + 32, 0, 8)

            gcT = gx[:, 3, :]
            with pool.Fori(0, NIT) as j:
                batch(j)
            if stop == "x2":
                return
            restart()
            pool.wait_ge(s_unit, U_FF)
            for m in braw + craw:
                link(nc.gpsimd.memset(m, 0.0))
            with nc.allow_non_contiguous_dma("small parameters"):
                pool.dma_start(araw[0:PAIRS, 0, :], A["a_re_2"][0].rearrange("(r g) p -> r (g p)", g=2)).then_inc(s_raw, 16)
                pool.dma_start(araw[0:PAIRS, 1, :], A["a_im_2"][0].rearrange("(r g) p -> r (g p)", g=2)).then_inc(s_raw, 16)
                pool.dma_start(ldraw[0:PAIRS, :], A["log_dt_2"][0].rearrange("(r g) -> r g", g=2)).then_inc(s_raw, 16)
                for c, nm in enumerate(("re", "im")):
                    for g in range(2):
                        pool.dma_start(braw[c][64 * g:64 * g + 64, :, 16 * g:16 * g + 16],
                                       A[f"b_{nm}_2"][0].rearrange("(r g) p c -> g p r c", g=2)[g]).then_inc(s_raw, 16)
                        for i in range(4):
                            q = 32 * i + 16 * g
                            pool.dma_start(craw[c][q:q + 16, :, 64 * g:64 * g + 64],
                                           A[f"c_{nm}_2"][0].rearrange("(t i g) c p -> i g c t p", i=4, g=2)[i, g])\
                                .then_inc(s_raw, 16)

            def tables(j, q):
                p = bass.ds(j * 8 + q, 1)
                c, s = (tabs[q % 2][:, i, :].rearrange("p (a b) -> p a b", a=16) for i in range(2))
                ta, tb_ = (ptmp[:, i, :].rearrange("p (a b) -> p a b", a=16) for i in range(2))
                big = lambda e: e[:, p, :].squeeze(1).unsqueeze(2).broadcast_to([P, 16, 16])
                small = lambda e: e[:, p, :].squeeze(1).unsqueeze(1).broadcast_to([P, 16, 16])
                tt = nc.gpsimd.tensor_tensor
                pool.wait_ge(s_tab, j * 8 + q)
                pool.wait_ge(s_h, j * 8 + (q + 1))
                tt(c, big(E16r), small(E1r), ALU.mult)
                link(tt(ta, big(E16i), small(E1i), ALU.mult))
                tt(s, big(E16r), small(E1i), ALU.mult)
                link(tt(tb_, big(E16i), small(E1r), ALU.mult))
                tt(c, c, ta, ALU.subtract)
                tt(s, s, tb_, ALU.add).then_inc(s_tab, 1)

            pool.wait_ge(s_vp, 2)
            pool.wait_ge(s_ap, 6)
            pool.wait_ge(s_uz, 4)
            with pool.Fori(0, 4) as j:
                restart()
                for q in range(8):
                    if q % 4 == 0:
                        i = q // 4
                        pool.wait_ge(s_yp, j * 8 + (4 * i + 4))
                        pool.wait_ge(s_yt, j * 2 + (i + 1))
                        t = bass.ds(j * 2 + i, 1)
                        nc.gpsimd.tensor_copy(ucur[i], uT[:, t, :].squeeze(1))
                        nc.gpsimd.tensor_copy(bcur[i], BC[:, t].squeeze(1)).then_inc(s_cur, 1)
                    tables(j, q)

        @block.tensor
        def _(pe):
            def tr(dst, src):
                n = src.shape[0]
                return nc.tensor.transpose(dst, src, ident[0:n, 0:n])

            pe.wait_ge(s_cst, N_CST)
            pe.wait_ge(s_vec, 16 * N_VEC)
            for t, n in enumerate(V_ROWS):
                m = tr(pd[0][:, t * P:t * P + n], vstage[0:n, t, :])
            m.then_inc(s_p0, 1)
            pe.wait_ge(s_x, 16)
            for kt in range(KD):
                b = kt // 4
                if kt == 12:
                    pe.wait_ge(s_a0, A0["vec"])
                for t in range(TT):
                    m = tr((pg + pd[::-1])[b][:, (kt % 4) * T + t * P:(kt % 4) * T + (t + 1) * P],
                           xtok[:, t, kt * P:(kt + 1) * P])
                if kt % 4 == 3:
                    m.then_inc(s_p0, 1)
            for ch in range(8):
                pe.wait_ge(s_acc, 4 * (ch + 1))
                if ch == 0:
                    pe.wait_ge(s_a0, A0["x3"])
                for q in range(4):
                    m = nc.tensor.matmul(pd[0][:, 4 * ch + q:4 * ch + q + 1], acc[:, ch % 2, q * P:(q + 1) * P],
                                         ones[:, 0:1], start=True, stop=True)
                m.then_inc(s_p0, 1)
            pe.wait_ge(s_v0, V0["h"])
            pe.wait_ge(s_wba, 48)
            for w in range(2):
                for k in range(KD):
                    m = nc.tensor.matmul(pd[1][0:NH, w * 512:w * 512 + T], wba[:, k, w * NH:(w + 1) * NH], hT[:, k, :],
                                         start=(k == 0), stop=(k == KD - 1))
            m.then_inc(s_p0, 1)
            pe.wait_ge(s_v0, V0["gc"])
            for n, (row, c) in enumerate(((3, 0), (3, 1), (2, 0), (2, 1), (0, 0))):
                m = tr(pd[0][:, 512 + n * NH:512 + (n + 1) * NH], gx[0:NH, row, c * P:(c + 1) * P])
            m.then_inc(s_p0, 1)

            def unit(slot, pair, kt0, first, last):
                for n in range(4):
                    for k in range(4):
                        yield nc.tensor.matmul(
                            pg[pair][:, n * T:(n + 1) * T], wr[slot][:, k, n * P:(n + 1) * P], hT[:, kt0 + k, :],
                            start=(first and k == 0 and n % 2 == 0), stop=(last and k == 3), skip_group_check=True)

            def gemm(g, base):
                for t in range(12):
                    slot, grp = t % 4, t // 4
                    pe.wait_ge(s_w[slot], g * 64 + 32 + 16 * grp)
                    if t == 0 and base:
                        pe.wait_ge(s_zo, g)
                    if t == 4 and base:
                        pe.wait_ge(s_cd, g * 2)
                    if t == 8:
                        pe.wait_ge(s_cd, g * 2 + 1)
                    for n, m in enumerate(unit(slot, grp % 2, 4 * slot, slot == 0, slot == 3)):
                        if n == 7:
                            yield
                    m.then_inc(s_unit, 1)
                    yield

            def pdv(i):
                return pd[i][:].rearrange("p (c h t) -> p c h t", c=TT, h=VH)

            def delta(it):
                bp, bv, ba, bg = it * len(PEO), it * len(VO), it * len(AO), it * len(GO)

                def V(name): pe.wait_ge(s_v, bv + VO[name])
                def Ac(name): pe.wait_ge(s_a, ba + AO0 + AO[name])
                pe.wait_ge(s_g, bg + GO["sq"])
                pe.wait_ge(s_v, bv)
                for n in range(2):
                    m = nc.tensor.matmul(pd[0][:, n * 512:(n + 1) * 512], ones[:], sqb[:, n * 512:(n + 1) * 512],
                                         start=True, stop=True)
                m.then_inc(s_pe, 1)
                pe.wait_ge(s_g, bg + GO["rowm"])
                for n in range(2):
                    m = nc.tensor.matmul(pd[1][:, n * 512:(n + 1) * 512], ones[0:NH, :],
                                         rowm[0:NH, n].rearrange("p a b -> p (a b)"), start=True, stop=True)
                m.then_inc(s_pe, 1)
                yield
                Ac("rn")
                for c in range(TT):
                    for h in range(VH):
                        m = tr(pdv(0)[:, c, h], vT[:, h, c * P:(c + 1) * P])
                m.then_inc(s_pe, 1)
                yield
                V("qkn")
                Ac("vtok")
                for w in range(2):
                    for c in range(TT):
                        for h in range(2):
                            m = nc.tensor.matmul(pd[0][:, w * 512 + (c * 2 + h) * P:w * 512 + (c * 2 + h + 1) * P],
                                                 qk[:, 2 + h, c * P:(c + 1) * P],
                                                 qk[:, (2 if w == 0 else 0) + h, c * P:(c + 1) * P],
                                                 start=True, stop=True)
                m.then_inc(s_pe, 1)
                V("dt")
                for h in range(2):
                    m = tr(pd[1][:, h * P:(h + 1) * P], qk[:, 2 + h, 0:P])
                m.then_inc(s_pe, 1)
                yield
                V("u2")
                Ac("kg")
                for n in range(8):
                    m = tr(pd[1][:, n * P:(n + 1) * P], Ub[:, n, :])
                m.then_inc(s_pe, 1)
                yield
                par = 0

                def x_step(s):
                    for n in range(8):
                        m = nc.tensor.matmul(pd[par][:, n * P:(n + 1) * P], lTb[:, n, :], Tb[:, n, :],
                                             start=True, stop=True)
                    m.then_inc(s_pe, 1)
                V("at")
                Ac("t2")
                x_step(2)
                yield
                for s in LEVELS:
                    V(f"x{s}")
                    if s > 2:
                        Ac(f"u{s // 2}")
                    par ^= 1
                    for n in range(8):
                        m = nc.tensor.matmul(pd[par][:, n * P:(n + 1) * P], Ub[:, n, :], Xb[:, n, :],
                                             start=True, stop=True)
                    m.then_inc(s_pe, 1)
                    yield
                    V(f"t{s}")
                    par ^= 1
                    for n in range(8):
                        m = tr(pd[par][:, n * P:(n + 1) * P], Tb[:, n, :])
                    m.then_inc(s_pe, 1)
                    par ^= 1
                    x_step(2 * s)
                    yield
                V("x64")
                Ac("u32")
                par ^= 1
                for n in range(8):
                    m = nc.tensor.matmul(pd[par][:, n * P:(n + 1) * P], Xb[:, n, :], Ub[:, n, :],
                                         start=True, stop=True)
                m.then_inc(s_pe, 1)
                assert par == 0
                yield
                V("u64")
                for h in range(VH):
                    m = nc.tensor.matmul(pd[1][:, h * P:(h + 1) * P], Ub[:, h, :], vtok[:, h, :], start=True, stop=True)
                m.then_inc(s_pe, 1)
                yield
                Ac("v0")
                for h in range(VH):
                    m = nc.tensor.matmul(pd[0][:, h * P:(h + 1) * P], kg0[:, h, :], vn0[:, h, :], start=True, stop=True)
                m.then_inc(s_pe, 1)
                for h in range(VH):
                    m = nc.tensor.matmul(pd[0][:, 512 + h * P:512 + (h + 1) * P], aTb[:, h, :], vn0[:, h, :],
                                         start=True, stop=True)
                m.then_inc(s_pe, 1)
                yield
                Ac("s")
                for h in range(VH):
                    m = nc.tensor.matmul(pd[1][:, h * P:(h + 1) * P], qk[:, 2 + h // 2, P:T], Sb[:, h, :],
                                         start=True, stop=True)
                m.then_inc(s_pe, 1)
                for h in range(VH):
                    m = nc.tensor.matmul(pd[1][:, 512 + h * P:512 + (h + 1) * P], qk[:, h // 2, P:T], Sb[:, h, :],
                                         start=True, stop=True)
                m.then_inc(s_pe, 1)
                yield
                V("rhs1")
                for h in range(VH):
                    m = nc.tensor.matmul(pd[0][:, h * P:(h + 1) * P], Ub[:, VH + h, :], rhs1[:, h, :],
                                         start=True, stop=True)
                m.then_inc(s_pe, 1)
                yield
                Ac("v1")
                Ac("qs")
                for h in range(VH):
                    m = nc.tensor.matmul(pd[1][:, h * P:(h + 1) * P], aTb[:, VH + h, :], vn1[:, h, :],
                                         start=True, stop=True)
                m.then_inc(s_pe, 1)
                yield
                V("on")
                for c in range(TT):
                    for h in range(VH):
                        m = tr(pdv(0)[:, c, h], ob[:, c * VH + h, :])
                m.then_inc(s_pe, 1)
                yield
                pe.wait_ge(s_acc, it * 8 + 40)
                for q in range(8):
                    m = nc.tensor.matmul(pd[1][:, q:q + 1], acc[:, q // 4, (q % 4) * P:(q % 4 + 1) * P],
                                         ones[:, 0:1], start=True, stop=True)
                m.then_inc(s_pe, 1)
                yield

            for _ in gemm(0, False):
                pass
            with pe.Fori(0, NIT - 1) as j:
                steps = delta(j)
                for _ in gemm(j + 1, True):
                    next(steps, None)
                for _ in steps:
                    pass
            for _ in delta(NIT - 1):
                pass

            def unit_at(u, slot, bank, rhs, first, last):
                pe.wait_ge(s_w[slot], W_GDN + (u - U_OUT) * 4 + 16 - 4 * slot)
                for n in range(4):
                    for k in range(4):
                        m = nc.tensor.matmul(bank[:, n * T:(n + 1) * T], wr[slot][:, k, n * P:(n + 1) * P], rhs(k),
                                             start=(first and k == 0 and n % 2 == 0), stop=(last and k == 3),
                                             skip_group_check=True)
                m.then_inc(s_unit, 1)

            def group(u, pair, rhs, n_units):
                for t in range(n_units):
                    unit_at(u + t, t % 4, pg[pair], lambda k: rhs[:, 4 * t + k, :], t == 0, t == n_units - 1)

            pe.wait_ge(s_v, NIT * len(VO))
            pe.wait_ge(s_zo, NIT)
            with pe.Fori(0, 2) as j:
                for i in range(2):
                    pe.wait_ge(s_ev, j * 2 + (i + 1))
                    group(j * 16 + (U_OUT + 8 * i), i, oT, 8)

            def mean(bank, ready, src):
                for c in range(4):
                    pe.wait_ge(*ready(c))
                    for k in range(4 * c, 4 * c + 4):
                        m = nc.tensor.matmul(bank[:, 0:T], onesd[:], src[:, k, :], start=(k == 0), stop=(k == KD - 1))
                m.then_inc(s_pn, 1)

            mean(pd[0], lambda c: (s_ev, 2 + c + 1), xT)
            mean(pd[1], lambda c: (s_an, AN["sqa"] + c), sqn)
            if stop != "x2":
                pe.wait_ge(s_raw, 16 * N_RAW)
                pe.wait_ge(s_an, AN["rsa"])
                pe.wait_ge(s_vx, 1)
                for c in range(3):
                    m = tr(pd[0][:, c * PAIRS:(c + 1) * PAIRS], araw[0:PAIRS, c, :])
                m.then_inc(s_pp, 1)
                for t in range(8):
                    m = tr(pd[1][:, t * P:(t + 1) * P], craw[1][:, t, :])
                m.then_inc(s_pp, 1)
                pe.wait_ge(s_ap, 1)
                for t in range(8):
                    m = tr(pd[0][:, t * P:(t + 1) * P], craw[0][:, t, :])
                m.then_inc(s_pp, 1)
            with pe.Fori(0, KF // 4) as j:
                for i in range(2):
                    if i == 0:
                        for t in range(4):
                            if t == 0:
                                pe.wait_ge(s_sg, j)
                            pe.wait_ge(s_vn, VN["ha"] + t)
                            unit_at(j * 8 + (U_FF + t), t, pg[0], lambda k: hT[:, 4 * t + k, :], t == 0, t == 3)
                    else:
                        pe.wait_ge(s_hg, j)
                        group(j * 8 + (U_FF + 4), 1, hT, 4)

            if stop != "x2":
                pe.wait_ge(s_vp, 1)
                for c in range(2):
                    for t in range(8):
                        m = tr(pd[c][:, t * P:(t + 1) * P], bbar[c][:, 4 * t:4 * t + 4, :].rearrange("p a b -> p (a b)"))
                m.then_inc(s_pp, 1)
                pe.wait_ge(s_ap, 6)
            banks = pg + pd

            def down(j, first, last):
                for t in range(4):
                    unit_at(j * 4 + (U_DOWN + t), t, banks[t], lambda k: hg[:, bass.ds(j * 4 + k, 1), :].squeeze(1),
                            first, last)
            pe.wait_ge(s_hg, KF // 4)
            down(0, True, False)
            with pe.Fori(1, KF // 4 - 1) as j:
                down(j, False, False)
            down(KF // 4 - 1, False, True)
            mean(pg[0], lambda c: (s_ev, G_DOWN + 2 + c + 1), xT)
            mean(pg[1], lambda c: (s_an, AN["sqb"] + c), sqn)
            mean(pd[0], lambda c: (s_an, AN["sqc"] + c), sqn)
            if stop == "x2":
                return

            with pe.Fori(0, 2) as j:
                for i in range(2):
                    pe.wait_ge(s_uz, j * 2)
                    for t in range(4):
                        pe.wait_ge(s_vn, VN["hc"] + t)
                        unit_at(j * 8 + (U_HYB + 4 * i + t), t, pg[i], lambda k: hT[:, 4 * t + k, :], t == 0, t == 3)

            def state_in(j, q):
                pe.wait_ge(s_cur, j * 2 + (q // 4 + 1))
                pe.wait_ge(s_h, j * 8 + (q + 1))
                r = slice(32 * (q % 4), 32 * (q % 4) + 32)
                for c in range(2):
                    m = nc.tensor.matmul(pd[0][:, (q % 2) * 512 + c * T:(q % 2) * 512 + (c + 1) * T],
                                         bcur[q // 4][r, c, :], ucur[q // 4][r, :], start=True, stop=True)
                m.then_inc(s_xp, 1)

            def state_out(j, q):
                pe.wait_ge(s_h, j * 8 + (q + 3))
                if q % 4 == 0:
                    pe.wait_ge(s_yt, j * 2 + (q // 4 + 1))
                r = slice(32 * (q % 4), 32 * (q % 4) + 32)
                for c in range(2):
                    m = nc.tensor.matmul(pd[1][r, (q // 4) * 512:(q // 4) * 512 + T], bcur[q // 4][:, 2 + c, r],
                                         hst[q % 2][:, c, :], start=(c == 0), stop=(c == 1))
                m.then_inc(s_yp, 1)

            pe.sem_inc(s_yp, 8)
            pe.wait_ge(s_uz, 4)
            with pe.Fori(0, 4) as j:
                for t in range(16):
                    if t == 0:
                        pe.wait_ge(s_bg, j)
                    if t == 4:
                        pe.wait_ge(s_za, j)
                    if t == 8:
                        pe.wait_ge(s_cg, j + 1)
                    if t == 12:
                        pe.wait_ge(s_vo, j + 1)
                    unit_at(j * 16 + (U_MIX + t), t % 4, pg[(t // 4) % 2], lambda k: hT[:, 4 * (t % 4) + k, :],
                            t % 4 == 0, t % 4 == 3)
                    if t % 2:
                        state_in(j, t // 2)
                        if t > 1:
                            state_out(j, t // 2 - 1)
                state_out(j, 7)
            pe.wait_ge(s_bg, 4)
            pe.wait_ge(s_za, 4)
            with pe.Fori(0, 4) as j:
                for i in range(2):
                    pe.wait_ge(s_gate, j * 2)
                    group(j * 8 + (U_GATE + 4 * i), i, hT, 4)
            pe.wait_ge(s_gate, 8)
            pe.wait_ge(s_gel, 1)
            for i in range(2):
                for t in range(2):
                    unit_at(U_GLU + 2 * i + t, 2 * i + t, pg[i], lambda k: yb[:, 4 * t + k, :], t == 0, t == 1)
            pe.wait_ge(s_ya, 4)
            pe.wait_ge(s_glu, 2)
            with pe.Fori(0, 2) as j:
                for i in range(2):
                    pe.wait_ge(s_m, j * 2 + i)
                    group(j * 8 + (U_OA + 4 * i), i, yaT, 4)
            pe.wait_ge(s_yg, 2)
            pe.wait_ge(s_m, 5)
            with pe.Fori(0, 2) as j:
                for i in range(2):
                    pe.wait_ge(s_m2, j * 2 + i)
                    for t in range(2):
                        unit_at(j * 4 + (U_OB + 2 * i + t), 2 * i + t, pg[i], lambda k: yg[:, 4 * t + k, :],
                                t == 0, t == 1)
            pe.wait_ge(s_m2, 5)
            with pe.Fori(0, 2) as j:
                for i in range(2):
                    pe.wait_ge(s_x3, j * 2 + i)
                    group(j * 8 + (U_O + 4 * i), i, mT, 4)
            mean(pd[0], lambda c: (s_an, AN["sqd"] + c), sqo)
            for t in range(TT):
                for b in range(4):
                    n = t * 4 + b
                    pe.wait_ge(s_vn, VN["xo"] + b)
                    if n >= 2:
                        pe.wait_ge(s_ao, n - 1)
                    for k in range(4):
                        m = tr(pg[n % 2][:, k * P:(k + 1) * P], xo[:, 4 * b + k, t * P:(t + 1) * P])
                    m.then_inc(s_po, 1)

        @block.scalar
        def _(act):
            link, restart = chain(act, s_aa)
            a = nc.scalar.activation
            act.wait_ge(s_p0, 1)
            for t in range(2):
                a(vc[:, t * 320:(t + 1) * 320], pd[0][:, t * 320:(t + 1) * 320], ACT.Copy).then_inc(s_a0, 1) if t == 0 else \
                    a(vc[:, 320:V_DSK + 8], pd[0][:, 320:V_DSK + 8], ACT.Copy).then_inc(s_a0, 1)
            act.wait_ge(s_a0, 2)
            a(condt[:], vc[:, V_C:V_C + KD], ACT.Silu).then_inc(s_a0, 1)
            for b in range(4):
                act.wait_ge(s_p0, 2 + b)
                a(xT[:, 4 * b:4 * b + 4, :].rearrange("p a b -> p (a b)"), (pg + pd[::-1])[b][:], ACT.Copy).then_inc(s_a0, 1)
            act.wait_ge(s_p0, 14)
            a(gx[0:NH, 2, :], pd[1][0:NH, 0:T], ACT.Sigmoid).then_inc(s_a0, 1)
            link(a(aT[0:NH], pd[1][0:NH, 512:512 + T], ACT.Identity, bias=alog[0:NH, 1:2]))
            link(a(bT[0:NH], aT[0:NH], ACT.Abs))
            nc.scalar.preload_act_table_set("natural_log_exp_and_others")
            link(a(bT[0:NH], bT[0:NH], ACT.Exp, scale=-1.0))
            a(bT[0:NH], bT[0:NH], ACT.Ln, bias=cst[0:NH, 3:4]).then_inc(s_a0, 1)
            a(alog[0:NH, 2:3], alog[0:NH, 0:1], ACT.Exp).then_inc(s_a0, 1)
            act.wait_ge(s_p0, 15)
            act.wait_ge(s_v0, V0["gc"])
            a(tk[:, 0:4, :].rearrange("p a b -> p (a b)"), pd[0][:, 512:512 + 4 * NH], ACT.Copy).then_inc(s_a0, 1)
            a(tk[:, 4, :], pd[0][:, 512 + NH:512 + 2 * NH], ACT.Exp).then_inc(s_a0, 1)
            a(tk[:, 6, :], pd[0][:, 512 + 4 * NH:512 + 5 * NH], ACT.Exp).then_inc(s_a0, 1)

            def tap(g, grp):
                act.wait_ge(s_unit, g * 12 + 4 * (grp + 1))
                for n in range(4):
                    a(pend[:, grp * 4 + n, :], pg[grp][:, n * T:(n + 1) * T], ACT.Copy,
                      scale=cwc[:, 3, grp * 4 + n:grp * 4 + n + 1]).then_inc(s_cv, 1)

            def z_out(g):
                act.wait_ge(s_unit, g * 12 + 12)
                a(zpend.rearrange("p a b -> p (a b)"), pg[0][:], ACT.Copy).then_inc(s_zo, 1)

            def silus(g, first):
                act.wait_ge(s_cd, g * 2 + 2)
                link(a(qk.rearrange("p a b -> p (a b)"), pend[:, 0:4, :].rearrange("p a b -> p (a b)"), ACT.Silu))
                a(vT.rearrange("p a b -> p (a b)"), pend[:, 4:8, :].rearrange("p a b -> p (a b)"), ACT.Silu).then_inc(s_a, 1)

            def silu_z(g):
                act.wait_ge(s_zo, g + 1)
                a(zT.rearrange("p a b -> p (a b)"), zpend.rearrange("p a b -> p (a b)"), ACT.Silu).then_inc(s_a, 1)

            def delta(it):
                bp, bv = it * len(PEO), it * len(VO)
                def PEw(name): act.wait_ge(s_pe, bp + PEO[name])
                def V(name): act.wait_ge(s_v, bv + VO[name])
                restart()
                nc.scalar.preload_act_table_set("natural_log_exp_and_others")
                PEw("ssq")
                link(a(rnb, pd[0][:], ACT.Ln, bias=cst[:, 0:1]))
                link(a(rnb[:, 0:512], rnb[:, 0:512], ACT.Exp, scale=-0.5, bias=cst[:, 2:3]))
                a(rnb[:, 512:1024], rnb[:, 512:1024], ACT.Exp, scale=-0.5).then_inc(s_a, 1)
                V("dt")
                a(dTb.rearrange("p a b -> p (a b)"), dTb.rearrange("p a b -> p (a b)"), ACT.Exp).then_inc(s_a, 1)
                PEw("vtok")
                a(vtok.rearrange("p a b -> p (a b)"), pd[0][:], ACT.Copy).then_inc(s_a, 1)
                yield
                PEw("ktok")
                for h in range(VH):
                    m = a(kg0[:, h, :], pd[1][:, (h // 2) * P:(h // 2 + 1) * P], ACT.Copy, scale=tkc[:, 6, h:h + 1])
                m.then_inc(s_a, 1)
                yield
                PEw("t2")
                a(Tb.rearrange("p a b -> p (a b)"), pd[1][:], ACT.Copy).then_inc(s_a, 1)
                yield
                par = 0
                for s in LEVELS:
                    PEw(f"u{s}")
                    a(Ub.rearrange("p a b -> p (a b)"), pd[par][:], ACT.Copy).then_inc(s_a, 1)
                    par ^= 1
                    yield
                PEw("v0")
                for h in range(VH):
                    m = a(vn0[:, h, :], pd[1][:, h * P:(h + 1) * P], ACT.Copy, scale=tkc[:, 2, h:h + 1])
                m.then_inc(s_a, 1)
                yield
                PEw("s")
                a(Sb.rearrange("p a b -> p (a b)"), pd[0][:, 0:512], ACT.Copy).then_inc(s_a, 1)
                yield
                PEw("qs")
                for h in range(VH):
                    m = a(ob[:, VH + h, :], pd[1][:, 512 + h * P:512 + (h + 1) * P], ACT.Copy, scale=tkc[:, 4, h:h + 1])
                m.then_inc(s_a, 1)
                PEw("v1")
                for h in range(VH):
                    m = a(vn1[:, h, :], pd[0][:, h * P:(h + 1) * P], ACT.Copy, scale=tkc[:, 3, h:h + 1])
                m.then_inc(s_a, 1)
                yield
                V("o1")
                for n in range(8):
                    link(a(Xb[:, n, :], ob[:, n, :], ACT.Square, accum_out=ssq[:, n:n + 1]))
                link(a(rstd, ssq, ACT.Ln, scale=1.0 / P, bias=cst[:, 0:1]))
                a(rstd, rstd, ACT.Exp, scale=-0.5).then_inc(s_a, 1)
                yield

            act.wait_ge(s_v0, V0["cw"])
            for grp in range(2):
                tap(0, grp)
            z_out(0)
            silus(0, True)
            silu_z(0)
            with act.Fori(0, NIT - 1) as j:
                steps = delta(j)
                for t in range(9):
                    next(steps)
                    if t == 4:
                        tap(j + 1, 0)
                    if t == 7:
                        tap(j + 1, 1)
                for _ in steps:
                    pass
                z_out(j + 1)
                silus(j + 1, False)
                act.wait_ge(s_v, j * len(VO) + VO["og"])
                silu_z(j + 1)
            for _ in delta(NIT - 1):
                pass

            def squares(ready):
                for c in range(4):
                    act.wait_ge(*ready(c))
                    a(sqn[:, 4 * c:4 * c + 4, :].rearrange("p a b -> p (a b)"),
                      xT[:, 4 * c:4 * c + 4, :].rearrange("p a b -> p (a b)"), ACT.Square).then_inc(s_an, 1)

            def inv_root(bank, n, eps):
                act.wait_ge(s_pn, n)
                restart()
                link(a(rs, bank[:, 0:T], ACT.Ln, bias=cst[:, eps:eps + 1]))
                a(rs, rs, ACT.Exp, scale=-0.5).then_inc(s_an, 1)

            def affine(g, b, ready):
                for c in range(4):
                    act.wait_ge(*ready(c))
                    for k in range(4 * c, 4 * c + 4):
                        m = a(xT[:, k, :], xT[:, k, :], ACT.Identity, scale=g[:, k:k + 1], bias=b[:, k:k + 1])
                    m.then_inc(s_an, 1)

            squares(lambda c: (s_vn, VN["da"] + c))
            inv_root(pd[1], 2, 1)
            affine(ag, ab, lambda c: (s_vn, VN["ha"] + c))
            if stop != "x2":
                act.wait_ge(s_pp, 1)
                a(prm[:, 0:3, :].rearrange("p a b -> p (a b)"), pd[0][:, 0:3 * PAIRS], ACT.Copy).then_inc(s_ap, 1)
                act.wait_ge(s_pp, 2)
                a(BC[:, :, 3, :], pd[1][:].rearrange("p (t s) -> p t s", s=P), ACT.Copy, scale=-1.0).then_inc(s_ap, 1)
                act.wait_ge(s_pp, 3)
                a(BC[:, :, 2, :], pd[0][:].rearrange("p (t s) -> p t s", s=P), ACT.Copy).then_inc(s_ap, 1)
                act.wait_ge(s_vx, 2)
                a(prm[:, 8, :], prm[:, 7, :], ACT.Sin)
                a(prm[:, 9, :], prm[:, 7, :], ACT.Sin, scale=0.5).then_inc(s_ap, 1)
            with act.Fori(0, KF // 4) as j:
                act.wait_ge(s_unit, j * 8 + (U_FF + 4))
                act.wait_ge(s_hg, j)
                a(sg.rearrange("p a b -> p (a b)"), pg[0][:], ACT.Silu).then_inc(s_sg, 1)
            if stop != "x2":
                act.wait_ge(s_pp, 4)
                for c in range(2):
                    a(BC[:, :, c, :], pd[c][:].rearrange("p (t s) -> p t s", s=P), ACT.Copy).then_inc(s_ap, 1)
            nc.scalar.preload_act_table_set("natural_log_exp_and_others")
            squares(lambda c: (s_vn, VN["db"] + c))
            inv_root(pg[1], 4, 1)
            for c in range(4):
                act.wait_ge(s_vn, VN["nb"] + c)
                for k in range(4 * c, 4 * c + 4):
                    m = a(xT[:, k, :], xT[:, k, :], ACT.Identity, scale=vc[:, V_LNG + KD + k:V_LNG + KD + k + 1],
                          bias=vc[:, V_LNB + KD + k:V_LNB + KD + k + 1])
                m.then_inc(s_an, 1)
            squares(lambda c: (s_an, AN["x2"] - 3 + c))
            inv_root(pd[0], 5, 0)
            if stop == "x2":
                return
            fl = lambda x: x.rearrange("p a b -> p (a b)")
            with act.Fori(0, 2) as j:
                act.wait_ge(s_unit, j * 8 + (U_HYB + 4))
                a(fl(uT[:, bass.ds(j * 4, 4), :]), pg[0][:], ACT.Copy).then_inc(s_uz, 1)
                act.wait_ge(s_unit, j * 8 + (U_HYB + 8))
                a(fl(zb[:, bass.ds(j * 4, 4), :]), pg[1][:], ACT.Silu).then_inc(s_uz, 1)
            with act.Fori(0, 4) as j:
                act.wait_ge(s_unit, j * 16 + (U_MIX + 4))
                act.wait_ge(s_vo, j)
                a(fl(cgb), pg[0][:], ACT.Copy).then_inc(s_cg, 1)
                act.wait_ge(s_vo, j + 1)
                act.wait_ge(s_ya, j)
                for n in range(4):
                    col = bass.ds(j * 4 + (V_CW2 + 2 * KD + n), 1)
                    m = a(cvb[:, n, :], pb[:, n, :], ACT.Copy, scale=vc[:, col])
                m.then_inc(s_tp, 1)
                act.wait_ge(s_unit, j * 16 + (U_MIX + 16))
                a(fl(szb), pg[1][:], ACT.Silu).then_inc(s_za, 1)
            act.wait_ge(s_yt, 10)
            a(fl(yb), fl(yb), ACT.Gelu_apprx_tanh).then_inc(s_gel, 1)
            with act.Fori(0, 4) as j:
                for i, dst in enumerate((sga, sgb)):
                    act.wait_ge(s_unit, j * 8 + (U_GATE + 4 * (i + 1)))
                    a(fl(dst[:, bass.ds(j * 4, 4), :]), pg[i][:], ACT.Sigmoid).then_inc(s_gate, 1)
            for i in range(2):
                act.wait_ge(s_unit, U_GLU + 2 * (i + 1))
                for n in range(4):
                    k = 4 * i + n
                    m = a(glu[:, k, :], pg[i][:, n * T:(n + 1) * T], ACT.Sigmoid, bias=vc[:, V_BGLU + k:V_BGLU + k + 1])
                m.then_inc(s_glu, 1)
            nc.scalar.preload_act_table_set("natural_log_exp_and_others")
            for c in range(4):
                act.wait_ge(s_x3, c + 2)
                a(fl(sqo[:, 4 * c:4 * c + 4, :]), fl(xT[:, 4 * c:4 * c + 4, :]), ACT.Square).then_inc(s_an, 1)
            inv_root(pd[0], 6, 0)
            for n in range(8):
                act.wait_ge(s_po, n + 1)
                a(ostage[n // 4][:, (n % 4) * 512:(n % 4 + 1) * 512], pg[n % 2][:, 0:512], ACT.Copy).then_inc(s_ao, 1)

        @block.vector
        def _(dve):
            v = nc.vector
            link, restart = chain(dve, s_vv)
            stt = v.scalar_tensor_tensor

            def mod_units(base, t0, n):
                for t in range(t0, t0 + n):
                    dve.wait_ge(s_mw[t % 2], base * 8 + 16 * (t // 2 + 1))
                    for k in range(4):
                        kk = (t % 4) * 4 + k
                        dst = acc[:, (t // 4) % 2, :]
                        if kk == 0:
                            m = v.tensor_scalar(dst, mw[t % 2][:, k, :], condt[:, kk:kk + 1], None, ALU.mult)
                        else:
                            m = stt(out=dst, in0=mw[t % 2][:, k, :], scalar=condt[:, kk:kk + 1], in1=dst,
                                    op0=ALU.mult, op1=ALU.add)
                        if k < 3:
                            link(m)
                    m.then_inc(s_acc, 1)
                    dve.wait_ge(s_acc, base + t + 1)

            dve.wait_ge(s_a0, A0["cond"])
            for ch in range(8):
                if ch >= 2:
                    dve.wait_ge(s_p0, 6 + ch - 1)
                mod_units(0, 4 * ch, 4)
            dve.wait_ge(s_p0, 13)
            dve.wait_ge(s_a0, A0["vec"])
            link(v.tensor_tensor(modt[:, 0:32], pd[0][:, 0:32], vc[:, V_MODB:V_MODB + 32], ALU.add))
            link(v.tensor_scalar(sc1p[:], modt[:, KD:2 * KD], 1.0, None, ALU.add))
            for k in range(KD):
                m = v.tensor_scalar(hT[:, k, :], xT[:, k, :], sc1p[:, k:k + 1], modt[:, k:k + 1], ALU.mult, ALU.add)
            m.then_inc(s_v0, 1)
            cwv = vc[:, V_CW:V_CW + 256].rearrange("p (a t) -> p a t", a=4)

            def taps(g):
                link(v.tensor_copy(cwc[:, :, 0:2], cwv[:, :, bass.ds(g * 2, 2)]))
                link(v.tensor_copy(cwc[:, :, 2:4], cwv[:, :, bass.ds(g * 2 + 16, 2)]))
                return v.tensor_copy(cwc[:, :, 4:8], cwv[:, :, bass.ds(g * 4 + 32, 4)])
            taps(0).then_inc(s_v0, 1)
            dve.wait_ge(s_a0, A0["sp"])
            gxv = lambda r: gx[0:NH, r, :]
            link(stt(out=gxv(1), in0=aT[0:NH], scalar=0.0, in1=bT[0:NH], op0=ALU.max, op1=ALU.add))
            link(v.tensor_scalar(gxv(1), gxv(1), alog[0:NH, 2:3], -1.0, ALU.mult, ALU.mult))
            link(v.memset(gxv(0), 1.0))
            for c in range(TT):
                link(v.tensor_tensor_scan(gx[0:NH, 3, c * P:(c + 1) * P], gx[0:NH, 0, c * P:(c + 1) * P],
                                          gx[0:NH, 1, c * P:(c + 1) * P], 0.0, ALU.mult, ALU.add))
            v.tensor_scalar(gx[0:NH, 0, 0:P], gx[0:NH, 3, 0:P], -1.0, gx[0:NH, 3, P - 1:P], ALU.mult, ALU.add)\
                .then_inc(s_v0, 1)
            dve.wait_ge(s_a0, A0["tok"])
            v.tensor_scalar(tk[:, 5, :], tk[:, 4, :], -1.0, None, ALU.mult).then_inc(s_v0, 1)

            def conv(g, grp):
                dve.wait_ge(s_cv, g * 8 + 4 * grp + 4)
                for sh in range(1, 4):
                    for n in range(4):
                        tile = grp * 4 + n
                        m = stt(out=pend[:, tile, sh:T], in0=pg[grp][:, n * T:(n + 1) * T - sh],
                                scalar=cwc[:, 3 - sh, tile:tile + 1], in1=pend[:, tile, sh:T],
                                op0=ALU.mult, op1=ALU.add)
                        if sh < 3 and n == 3:
                            link(m)
                m.then_inc(s_cd, 1)

            def bc_heads(m):
                return m[:].unsqueeze(1).broadcast_to([P, 8, P])

            def delta(it, mods):
                bp, ba, bv = it * len(PEO), it * len(AO), it * len(VO)
                def PEw(name): dve.wait_ge(s_pe, bp + PEO[name])
                def Ac(name): dve.wait_ge(s_a, ba + AO0 + AO[name])
                def done(m): m.then_inc(s_v, 1)
                restart()
                dve.wait_ge(s_v0, V0["tok"])
                link(v.tensor_copy(tkc, tk[:, :, bass.ds(it * VH, VH)]))
                if mods:
                    done(taps(it + 1))
                else:
                    done(v.tensor_copy(cwc[:, 0, 0:1], cwc[:, 0, 0:1]))
                Ac("rn")
                done(v.tensor_tensor(qk.rearrange("p a b -> p (a b)"), qk.rearrange("p a b -> p (a b)"), rnb, ALU.mult))
                PEw("rows")
                for c in range(TT):
                    for h in range(VH):
                        n = c * VH + h
                        m = stt(out=dTb[:, n, :], in0=pd[1][:, n * P:(n + 1) * P], scalar=tkc[:, c, h:h + 1], in1=mneg[:],
                                op0=ALU.subtract, op1=ALU.min)
                done(m)
                yield
                PEw("gram")
                Ac("exp")
                for c in range(TT):
                    for h in range(VH):
                        n, b = c * VH + h, c * 2 + h // 2
                        m = stt(out=lTb[:, n, :], in0=pd[0][:, b * P:(b + 1) * P], scalar=tkc[:, 2 + c, h:h + 1],
                                in1=dTb[:, n, :], op0=ALU.mult, op1=ALU.mult)
                done(m)
                for b in range(4):
                    m = v.tensor_tensor(aTb[:, 2 * b:2 * b + 2, :],
                                        pd[0][:, 512 + b * P:512 + (b + 1) * P].unsqueeze(1).broadcast_to([P, 2, P]),
                                        dTb[:, 2 * b:2 * b + 2, :], ALU.mult)
                done(m)
                dve.wait_ge(s_v, bv + VO["lt"])
                link(v.tensor_tensor(Ub, lTb, bc_heads(m1t), ALU.mult))
                done(v.tensor_tensor(Ub, bc_heads(ident), Ub, ALU.subtract))
                yield
                par = 0
                Xf, Tf, Uf = (b.rearrange("p a b -> p (a b)") for b in (Xb, Tb, Ub))
                for s in LEVELS:
                    PEw(f"x{s}")
                    done(v.tensor_tensor(Xb, pd[par][:].rearrange("p (a b) -> p a b", b=P), bc_heads(msk[s]), ALU.mult))
                    par ^= 1
                    yield
                    PEw(f"tx{s}")
                    done(v.tensor_tensor(Tf, Tf, pd[par][:], ALU.subtract))
                    if s == 2:
                        pass
                    par ^= 1
                    par ^= 1
                    yield
                PEw("x64")
                done(v.tensor_tensor(Xb, pd[par][:].rearrange("p (a b) -> p a b", b=P), bc_heads(msk[64]), ALU.mult))
                yield
                PEw("ux64")
                done(v.tensor_tensor(Uf, Uf, pd[0][:], ALU.subtract))
                yield
                PEw("o0")
                done(v.tensor_copy(ob[:, 0:VH, :].rearrange("p a b -> p (a b)"), pd[0][:, 512:1024]))
                yield
                PEw("r")
                for h in range(VH):
                    m = stt(out=rhs1[:, h, :], in0=pd[1][:, h * P:(h + 1) * P], scalar=tkc[:, 5, h:h + 1],
                            in1=vtok[:, VH + h, :], op0=ALU.mult, op1=ALU.add)
                done(m)
                yield
                PEw("o1")
                done(v.tensor_tensor(ob[:, VH:8, :].rearrange("p a b -> p (a b)"),
                                     ob[:, VH:8, :].rearrange("p a b -> p (a b)"), pd[1][:, 0:512], ALU.add))
                Ac("rstd")
                done(v.tensor_tensor(ob, ob, rstd.unsqueeze(2).broadcast_to([P, 8, P]), ALU.mult))
                yield

            def finish(it):
                def PEw(name): dve.wait_ge(s_pe, it * len(PEO) + PEO[name])
                PEw("otr")
                dve.wait_ge(s_a, it * len(AO) + AO0)
                for c in range(TT):
                    m = stt(out=oT[:, bass.ds(it * VH, VH), c * P:(c + 1) * P],
                            in0=pd[0][:, c * 512:(c + 1) * 512].rearrange("p (h t) -> p h t", h=VH),
                            scalar=vc[:, V_NW:V_NW + 1], in1=zT[:, :, c * P:(c + 1) * P], op0=ALU.mult, op1=ALU.mult)
                m.then_inc(s_v, 1)
                PEw("mod")
                v.tensor_tensor(modt[:, bass.ds(it * 8 + 32, 8)], pd[1][:, 0:8],
                                vc[:, bass.ds(it * 8 + V_MODB + 32, 8)], ALU.add).then_inc(s_v, 1)

            for grp in range(2):
                conv(0, grp)
            with dve.Fori(0, NIT - 1) as j:
                steps = delta(j, True)
                for t in range(18):
                    next(steps, None)
                    if t == 5:
                        conv(j + 1, 0)
                    if t == 13:
                        conv(j + 1, 1)
                    if t % 2 and t < 16:
                        mod_units(j * 8 + 32, t // 2, 1)
                finish(j)
            steps = delta(NIT - 1, False)
            for t in range(18):
                next(steps, None)
                if t % 2 and t < 16:
                    mod_units(NIT * 8 + 24, t // 2, 1)
            finish(NIT - 1)
            restart()
            dve.wait_ge(s_v, NIT * len(VO))
            lng, lnb = vc[:, V_LNG:V_LNG + KD], vc[:, V_LNB:V_LNB + KD]
            link(v.tensor_scalar(ga1p, modt[:, 2 * KD:3 * KD], 1.0, None, ALU.add))
            link(v.tensor_scalar(sc2p, modt[:, 4 * KD:5 * KD], 1.0, None, ALU.add))
            link(v.tensor_tensor(g1, lng, sc2p, ALU.mult))
            link(v.tensor_tensor(b1, lnb, sc2p, ALU.mult))
            link(v.tensor_tensor(b1, b1, modt[:, 3 * KD:4 * KD], ALU.add))
            link(v.tensor_scalar(ag, lng, ALPHA, None, ALU.mult))
            link(v.tensor_scalar(ab, lnb, ALPHA, None, ALU.mult))
            link(v.tensor_scalar(ga2p, modt[:, 5 * KD:6 * KD], 1.0, None, ALU.add))
            link(v.tensor_scalar(xT[:], xT[:], ALPHA, None, ALU.mult))
            dve.sem_inc(s_ev, 2)

            def residual(j, pair, fac):
                for n in range(4):
                    k = bass.ds(j * 4 + n, 1)
                    m = stt(out=xT[:, k, :].squeeze(1), in0=pair[:, n * T:(n + 1) * T], scalar=fac[:, k],
                            in1=xT[:, k, :].squeeze(1), op0=ALU.mult, op1=ALU.add)
                m.then_inc(s_ev, 1)

            def centre(bank, n):
                dve.wait_ge(s_pn, n)
                for c in range(4):
                    v.tensor_tensor(xT[:, 4 * c:4 * c + 4, :], xT[:, 4 * c:4 * c + 4, :],
                                    bank[:, 0:T].unsqueeze(1).broadcast_to([P, 4, T]), ALU.subtract).then_inc(s_vn, 1)

            with dve.Fori(0, 2) as j:
                for i in range(2):
                    dve.wait_ge(s_unit, j * 16 + (U_OUT + 8 * (i + 1)))
                    residual(j * 2 + i, pg[i], ga1p)
            dve.wait_ge(s_ev, 6)
            centre(pd[0], 1)
            dve.wait_ge(s_an, AN["rsa"])
            for c in range(4):
                if c == 0:
                    dve.wait_ge(s_vn, VN["da"] + 3)
                t4 = xT[:, 4 * c:4 * c + 4, :]
                link(v.tensor_tensor(t4, t4, rs.unsqueeze(1).broadcast_to([P, 4, T]), ALU.mult))
                for k in range(4 * c, 4 * c + 4):
                    m = v.tensor_scalar(hT[:, k, :], xT[:, k, :], g1[:, k:k + 1], b1[:, k:k + 1], ALU.mult, ALU.add)
                m.then_inc(s_vn, 1)
            def state_parameters():
                restart()
                dve.wait_ge(s_raw, 16 * N_RAW)
                ts, tt = v.tensor_scalar, v.tensor_tensor
                v.tensor_copy(araw[0:PAIRS, 2, :].rearrange("p (g q) -> p g q", g=2),
                              ldraw[0:PAIRS, :].unsqueeze(2).broadcast_to([PAIRS, 2, 64])).then_inc(s_vx, 1)
                dve.wait_ge(s_ap, 1)
                col = lambda i: prm[:, i, :]
                are, aim, ldt, dt, xr, th, r, phi, sn, sh, tA, tB, tC, tD, cs, den = (col(i) for i in range(16))
                tint = col(16).bitcast(mybir.dt.int32)

                def mul(o, x, y): link(tt(o, x, y, ALU.mult))

                def exp(o, x):
                    link(ts(tA, x, -104.0, 89.0, ALU.max, ALU.min))
                    link(ts(tB, tA, 1.0 / math.log(2.0), MAGIC, ALU.mult, ALU.add))
                    link(ts(tB, tB, MAGIC, None, ALU.subtract))
                    link(stt(out=tA, in0=tB, scalar=-LN2_HI, in1=tA, op0=ALU.mult, op1=ALU.add))
                    link(stt(out=tA, in0=tB, scalar=-LN2_LO, in1=tA, op0=ALU.mult, op1=ALU.add))
                    link(ts(tC, tA, 1.0 / math.factorial(8), None, ALU.mult))
                    for n in range(7, 0, -1):
                        link(stt(out=tC, in0=tC, scalar=1.0 / math.factorial(n), in1=tA, op0=ALU.add, op1=ALU.mult))
                    link(ts(tB, tB, 127.0, 0.0, ALU.add, ALU.max))
                    link(ts(tint, tB, 8388608.0, None, ALU.mult))
                    link(stt(out=o, in0=tC, scalar=1.0, in1=col(16), op0=ALU.add, op1=ALU.mult))

                exp(dt, ldt)
                mul(xr, are, dt)
                mul(th, aim, dt)
                exp(rdec, xr)
                link(ts(tB, th, 1.0 / (2 * math.pi), MAGIC, ALU.mult, ALU.add))
                link(ts(tB, tB, MAGIC, None, ALU.subtract))
                link(stt(out=th, in0=tB, scalar=-TURN[0], in1=th, op0=ALU.mult, op1=ALU.add))
                link(stt(out=th, in0=tB, scalar=-TURN[1], in1=th, op0=ALU.mult, op1=ALU.add))
                link(stt(out=th, in0=tB, scalar=-TURN[2], in1=th, op0=ALU.mult, op1=ALU.add))
                ts(phi, th, 3.1415925, -3.1415925, ALU.min, ALU.max).then_inc(s_vx, 1)
                dve.wait_ge(s_ap, 4)
                link(stt(out=tD, in0=sh, scalar=-2.0, in1=sh, op0=ALU.mult, op1=ALU.mult))
                link(ts(cs, tD, 1.0, None, ALU.add))
                link(stt(out=tA, in0=rdec, scalar=-1.0, in1=cs, op0=ALU.add, op1=ALU.mult))
                link(tt(tA, tA, tD, ALU.add))
                mul(tB, rdec, sn)
                mul(den, are, are)
                mul(tC, aim, aim)
                link(tt(den, den, tC, ALU.add))
                link(v.reciprocal(den, den))
                mul(tC, tA, are)
                mul(tD, tB, aim)
                link(tt(tC, tC, tD, ALU.add))
                mul(xr, tC, den)
                mul(tC, tB, are)
                mul(tD, tA, aim)
                link(tt(tC, tC, tD, ALU.subtract))
                mul(r, tC, den)
                wide = lambda x: x.unsqueeze(2).broadcast_to([P, PAIRS, 32])
                mul(bbar[0], braw[0], wide(xr))
                mul(btmp, braw[1], wide(r))
                link(tt(bbar[0], bbar[0], btmp, ALU.subtract))
                mul(bbar[1], braw[1], wide(xr))
                mul(btmp, braw[0], wide(r))
                tt(bbar[1], bbar[1], btmp, ALU.add).then_inc(s_vp, 1)
                for er, ei in ((E1r, E1i), (E16r, E16i)):
                    link(v.memset(er[:, :, 0:1], 1.0))
                    link(v.memset(ei[:, :, 0:1], 0.0))
                    n = 1
                    while n < 16:
                        w = lambda x: x.unsqueeze(2).broadcast_to([P, PAIRS, n])
                        t0, t1 = (btmp[:, :, 8 * i:8 * i + n] for i in range(2))
                        mul(t0, er[:, :, 0:n], w(cs))
                        mul(t1, ei[:, :, 0:n], w(sn))
                        link(tt(er[:, :, n:2 * n], t0, t1, ALU.subtract))
                        mul(t0, er[:, :, 0:n], w(sn))
                        mul(t1, ei[:, :, 0:n], w(cs))
                        link(tt(ei[:, :, n:2 * n], t0, t1, ALU.add))
                        mul(tA, sn, sn)
                        mul(tB, cs, sn)
                        mul(cs, cs, cs)
                        link(tt(cs, cs, tA, ALU.subtract))
                        link(ts(sn, tB, 2.0, None, ALU.mult))
                        n *= 2
                v.memset(tA, 0.0).then_inc(s_vp, 1)

            if stop != "x2":
                state_parameters()
            with dve.Fori(0, KF // 4) as j:
                dve.wait_ge(s_unit, j * 8 + (U_FF + 8))
                dve.wait_ge(s_sg, j + 1)
                v.tensor_tensor(hg[:, bass.ds(j * 4, 4), :].rearrange("p a b -> p (a b)"),
                                sg.rearrange("p a b -> p (a b)"), pg[1][:], ALU.mult).then_inc(s_hg, 1)
            dve.wait_ge(s_an, AN["x1"])
            for i in range(4):
                dve.wait_ge(s_unit, U_DOWN + KF - 3 + i)
                residual(i, (pg + pd)[i], ga2p)
            dve.wait_ge(s_ev, G_DOWN + 6)
            centre(pg[0], 3)
            dve.wait_ge(s_an, AN["rsb"])
            for c in range(4):
                if c == 0:
                    dve.wait_ge(s_vn, VN["db"] + 3)
                t4 = xT[:, 4 * c:4 * c + 4, :]
                v.tensor_tensor(t4, t4, rs.unsqueeze(1).broadcast_to([P, 4, T]), ALU.mult).then_inc(s_vn, 1)
            dve.wait_ge(s_an, AN["rsc"])
            for k in range(KD):
                m = stt(out=hT[:, k, :], in0=xT[:, k, :], scalar=vc[:, V_NG + k:V_NG + k + 1], in1=rs,
                        op0=ALU.mult, op1=ALU.mult)
                if k % 4 == 3:
                    m.then_inc(s_vn, 1)

            if stop == "x2":
                return

            def pair(j, q):
                dve.wait_ge(s_h, j * 8 + (q + 2))
                dve.wait_ge(s_xp, j * 8 + (q + 1))
                dve.wait_ge(s_tab, j * 8 + (q + 1))
                c, sn = (tabs[q % 2][:, i, :].unsqueeze(1).broadcast_to([P, 2, T]) for i in range(2))
                x = pd[0][:, (q % 2) * 512:(q % 2 + 1) * 512].rearrange("p (a b) -> p a b", a=2)
                tt = v.tensor_tensor
                tt(p1, x, c, ALU.mult)
                link(tt(p2, x, sn, ALU.mult))
                tt(p1[:, 0, :], p1[:, 0, :], p2[:, 1, :], ALU.add)
                link(tt(p1[:, 1, :], p1[:, 1, :], p2[:, 0, :], ALU.subtract))
                dec = rdec[:, bass.ds(j * 8 + q, 1)].broadcast_to([P, T])
                for i in range(2):
                    m = v.tensor_tensor_scan(gst[:, i, :], dec, p1[:, i, :], 0.0, ALU.mult, ALU.add)
                link(m)
                tt(p1, gst, c, ALU.mult)
                link(tt(p2, gst, sn, ALU.mult))
                dve.wait_ge(s_yp, j * 8 + (q + 7))
                h = hst[q % 2]
                tt(h[:, 0, :], p1[:, 0, :], p2[:, 1, :], ALU.subtract)
                tt(h[:, 1, :], p1[:, 1, :], p2[:, 0, :], ALU.add).then_inc(s_h, 1)

            def tile_out(j, i):
                dve.wait_ge(s_yp, j * 8 + (12 + 4 * i))
                t = bass.ds(j * 2 + i, 1)
                stt(out=yb[:, t, :].squeeze(1), in0=ucur[i], scalar=vc[:, bass.ds(j * 2 + (V_DSK + i), 1)],
                    in1=pd[1][:, i * 512:i * 512 + T], op0=ALU.mult, op1=ALU.add).then_inc(s_yt, 1)

            fl = lambda x: x.rearrange("p a b -> p (a b)")
            dve.sem_inc(s_h, 2)
            dve.sem_inc(s_yt, 2)
            dve.sem_inc(s_m, 1)
            dve.sem_inc(s_m2, 1)
            dve.sem_inc(s_x3, 1)
            with dve.Fori(0, 4) as j:
                restart()
                for q in range(4):
                    pair(j, q)
                dve.wait_ge(s_cg, j + 1)
                dve.wait_ge(s_unit, j * 16 + (U_MIX + 8))
                v.tensor_tensor(fl(pb), fl(cgb), pg[1][:], ALU.mult).then_inc(s_vo, 1)
                pair(j, 4)
                dve.wait_ge(s_tp, j + 1)
                for sh in (1, 2):
                    for n in range(4):
                        m = stt(out=cvb[:, n, sh:T], in0=pb[:, n, 0:T - sh],
                                scalar=vc[:, bass.ds(j * 4 + (V_CW2 + (2 - sh) * KD + n), 1)], in1=cvb[:, n, sh:T],
                                op0=ALU.mult, op1=ALU.add)
                    link(m)
                pair(j, 5)
                tile_out(j, 0)
                dve.wait_ge(s_unit, j * 16 + (U_MIX + 12))
                v.tensor_tensor(fl(cvb), fl(cvb), pg[0][:], ALU.mult).then_inc(s_bg, 1)
                dve.wait_ge(s_bg, j + 1)
                pair(j, 6)
                pair(j, 7)
                dve.wait_ge(s_za, j + 1)
                v.tensor_tensor(fl(yaT[:, bass.ds(j * 4, 4), :]), fl(cvb), fl(szb), ALU.mult).then_inc(s_ya, 1)
                tile_out(j, 1)
            for i in range(2):
                k = slice(4 * i, 4 * i + 4)
                restart()
                dve.wait_ge(s_glu, i + 1)
                if i == 0:
                    dve.wait_ge(s_gel, 1)
                link(v.tensor_tensor(fl(glu[:, k, :]), fl(glu[:, k, :]), fl(yb[:, k, :]), ALU.mult))
                v.tensor_tensor(fl(yg[:, k, :]), fl(glu[:, k, :]), fl(zb[:, k, :]), ALU.mult).then_inc(s_yg, 1)
            dve.wait_ge(s_gate, 8)
            with dve.Fori(0, 2) as j:
                for i in range(2):
                    dve.wait_ge(s_unit, j * 8 + (U_OA + 4 * (i + 1)))
                    t4 = fl(sga[:, bass.ds(j * 8 + 4 * i, 4), :])
                    v.tensor_tensor(t4, t4, pg[i][:], ALU.mult).then_inc(s_m, 1)
            dve.wait_ge(s_m, 5)
            with dve.Fori(0, 2) as j:
                for i in range(2):
                    restart()
                    dve.wait_ge(s_unit, j * 4 + (U_OB + 2 * (i + 1)))
                    ta, tb = (fl(x[:, bass.ds(j * 8 + 4 * i, 4), :]) for x in (sga, sgb))
                    link(v.tensor_tensor(tb, tb, pg[i][:], ALU.mult))
                    v.tensor_tensor(ta, ta, tb, ALU.add).then_inc(s_m2, 1)
            with dve.Fori(0, 2) as j:
                for i in range(2):
                    dve.wait_ge(s_unit, j * 8 + (U_O + 4 * (i + 1)))
                    t4 = fl(xT[:, bass.ds(j * 8 + 4 * i, 4), :])
                    v.tensor_tensor(t4, t4, pg[i][:], ALU.add).then_inc(s_x3, 1)
            dve.wait_ge(s_x3, 5)
            dve.wait_ge(s_an, AN["rsd"])
            for k in range(KD):
                m = stt(out=xo[:, k, :], in0=xT[:, k, :], scalar=vc[:, V_FG + k:V_FG + k + 1], in1=rs,
                        op0=ALU.mult, op1=ALU.mult)
                if k % 4 == 3:
                    m.then_inc(s_vn, 1)


_INS = ["x", "c", "mod_w", "mod_b", "ln_g", "ln_b", "ffn_w_gu", "ffn_w_down", "gdn_w_in", "gdn_conv_w", "gdn_a_log",
        "gdn_dt_bias", "gdn_norm_w", "gdn_w_out", "norm_g_2", "w_in_2", "conv_w_2", "w_out_a_2", "a_re_2", "a_im_2",
        "log_dt_2", "b_re_2", "b_im_2", "c_re_2", "c_im_2", "d_skip_2", "w_glu_2", "b_glu_2", "w_out_b_2", "w_o_2",
        "final_g_2"]


def kernel(**inputs):
    import numpy as np
    import concourse.bacc as bacc
    from concourse.bass_utils import run_bass_kernel_spmd

    nc = bacc.Bacc("TRN2", target_bir_lowering=False, num_devices=1)
    arrays, views = {}, {}
    for name in _INS:
        a = np.ascontiguousarray(inputs[name])
        arrays[f"in_{name}"] = a
        views[name] = nc.dram_tensor(f"in_{name}", a.shape, mybir.dt.from_np(a.dtype), kind="ExternalInput").ap()
    out = nc.dram_tensor("out", (1, T, D), F32, kind="ExternalOutput").ap()
    build(nc, views, out)
    r = run_bass_kernel_spmd(nc, [arrays], core_ids=[0])
    return r.results[0]["out"]
```

```python
import math
from contextlib import ExitStack

import concourse.bass as bass
import concourse.mybir as mybir

F32 = mybir.dt.float32
F32R = mybir.dt.float32r
ALU = mybir.AluOpType
ACT = mybir.ActivationFunctionType

P = 128
T = 256
TT = T // P
D = 2048
KD = D // P
NH = 32
NQK = 16
NIT = NQK // 2
VH = 4
GQ, GK, GV, GZ, GB, GA = 0, 2048, 4096, 8192, 12288, 12320
FF = 5632
KF = FF // P
PAIRS = 32
ALPHA = 2.0 ** 0.25
LN_EPS = 1e-5
EPS = 1e-6
LEVELS = (2, 4, 8, 16, 32)
BIG = -1.0e30

V_MODB, V_C, V_FG = 0, 96, 112
V_LNG, V_LNB, V_NG, V_CW2 = 128, 160, 192, 208
V_CW = 256
V_NW, V_BGLU, V_DSK = 512, 513, 521
V_ROWS = (128, 128, 128, 128, 17)

def order(*names):
    return {n: i + 1 for i, n in enumerate(names)}


PEO = order("ssq", "rows", "vtok", "gram", "ktok", "t2", "x2", "tx2", "u2", "x4", "tx4", "u4", "x8",
            "tx8", "u8", "x16", "tx16", "u16", "x32", "tx32", "u32", "x64", "ux64", "v0", "s", "o0", "r",
            "qs", "v1", "o1", "otr", "mod")
VO = order("scal", "qkn", "dt", "lt", "at", "u2", *[f"{a}{s}" for s in LEVELS for a in ("x", "t")],
           "x64", "u64", "o0", "rhs1", "o1", "on", "og", "modt")
AO = order("rn", "exp", "vtok", "kg", "t2", *[f"u{s}" for s in LEVELS], "v0", "s", "qs", "v1",
           "rstd", "qkv", "z")
GO = order("sq", "rowm")


LN_QSCALE = -0.5 * math.log(128.0)
N_VEC = 12
U_OUT = 12 * NIT + 12
CK_FF = 40
CK_FB = CK_FF + 16
CK_FD = CK_FB + 24 * (KF // 4 - 1)
CK_HYB = CK_FD + 8
CK_MIX = CK_HYB + 32
CK_GA = CK_MIX + 128
CK_GLU = CK_GA + 8
CK_TAIL = CK_GLU + 8
CK_LAST = CK_TAIL + 3 * 28
CK_O = CK_LAST + 20
CK_END = CK_O + 32
PARTS_FIRST = 2
AHEAD = 3
W_MOD = 128
W_GDN = W_MOD + 64 * NIT + 48




O_ORDER = (6, 7, 0, 1, 2, 3, 4, 5)


def out_chunk(t):
    if t < 8:
        return t // 4, 12 + t % 4, t % 4 == 3
    return 2 + (t - 8) // 16, (t - 8) % 16, (t - 8) % 16 == 15


def o_ready(k):
    return O_ORDER.index(k // 4) + 1


def first_of(*runs):
    at, n = {}, 0
    for name, count in runs:
        at[name] = n + 1
        n += count
    return at


AN = first_of(("sqa", 4), ("rsa", 1), ("x1_", 4), ("sqb", 4), ("rsb", 1), ("x2_", 4), ("sqc", 4), ("rsc", 1),
              ("sqd", 4), ("rsd", 1))
AN["x1"], AN["x2"] = AN["x1_"] + 3, AN["x2_"] + 3
VN = first_of(("da", 4), ("ha", 4), ("db", 4), ("nb", 4), ("hc", 4), ("xo", 4))
C_V, C_BG, C_CG, C_ZA, C_U, C_ZB, C_GA, C_GB = 0, 2048, 4096, 6144, 8192, 9216, 10240, 12288
N_RAW = 3 + 2 * 2 * 5
MAGIC = 12582912.0
LN2_HI = 0.693359375
LN2_LO = math.log(2.0) - LN2_HI
TURN = (6.28125, 0.0019350051879882812, 2 * math.pi - 6.28125 - 0.0019350051879882812)
AO0 = 2
N_CST = 2 + 4 + 1 + 1 + 7
A0 = {"vec": 2, "cond": 3, "x3": 7, "beta": 8, "sp": 10, "tok": 13}
V0 = {"h": 1, "cw": 2, "gc": 3, "tok": 4}


def build(nc, A, out):
    ctx = ExitStack()
    with ctx:
        def sb(name, shape, dt=F32):
            return ctx.enter_context(nc.sbuf_tensor(name, shape, dt))

        def sem(name):
            return ctx.enter_context(nc.semaphore(name))

        ident = sb("ident", [P, P])
        ones = sb("ones", [P, P])
        onesd = sb("onesd", [P, P])
        mneg = sb("mneg", [P, P])
        m1t = sb("m1t", [P, P])
        masks = sb("masks", [P, 6, P])
        msk = {s: masks[:, i, :] for i, s in enumerate(LEVELS + (64,))}
        vc = sb("vc", [P, 640])
        modt = sb("modt", [P, 96])
        cst = sb("cst", [P, 4])
        sc1p = sb("sc1p", [P, KD])
        condt = sb("condt", [P, KD])
        xT = sb("xT", [P, KD, T])
        h_at = nc.sbuf_base
        hT = sb("hT", [P, KD, T])
        w_at = [nc.sbuf_base]
        wr = [sb("wr0", [P, 4, 512])]
        for i in (1, 2, 3):
            w_at.append(nc.sbuf_base)
            wr.append(sb(f"wr{i}", [P, 4, 512]))
        ARENA = 34300
        arena_at = nc.sbuf_base
        arena = sb("arena", [P, ARENA])
        at = [0]

        def take(*shape):
            n = 1
            for s in shape:
                n *= s
            v = arena[:, at[0]:at[0] + n]
            at[0] += n
            assert at[0] <= ARENA, at
            names = "abcd"[:len(shape)]
            return v.rearrange(f"p ({' '.join(names)}) -> p {' '.join(names)}",
                               **{k: s for k, s in zip(names[:-1], shape[:-1])}) if len(shape) > 1 else v

        oT = take(NH, T)
        xtok = oT[:, 0:16, :].rearrange("p a b -> p (a b)").rearrange("p (t n) -> p t n", t=TT)
        vstage = oT[:, 16:19, :].rearrange("p a b -> p (a b)")[:, 0:640].rearrange("p (t n) -> p t n", t=5)
        mw = [take(4, 512) for _ in range(2)]
        acc = take(2, 512)
        acc2 = mw[0][:, 0:2, :]
        pend = take(8, T)
        zpend = take(VH, T)
        qk = take(4, T)
        vT = take(VH, T)
        zT = take(VH, T)
        Xb = take(8, P)
        Tb = take(8, P)
        Ub = take(8, P)
        sqb = Xb.rearrange("p a b -> p (a b)")
        rnb = Tb.rearrange("p a b -> p (a b)")
        dTb = take(8, P)
        lTb = take(8, P)
        aTb = take(8, P)
        vtok = take(8, P)
        kg0 = take(VH, P)
        vn0 = take(VH, P)
        vn1 = take(VH, P)
        Sb = take(VH, P)
        rhs1 = take(VH, P)
        ob = take(8, P)
        rowm = take(2, VH, P)
        tk = take(7, NH)
        tkc = take(7, VH)
        cwc = take(4, 8)
        ssq = take(8)
        rstd = take(8)
        bT = take(T)
        aT = take(T)
        wba = lTb.rearrange("p a b -> p (a b)").rearrange("p (k n) -> p k n", k=KD)
        gx = take(4, T)
        alog = take(4)

        def over(name, byte, *shape):
            return nc.alloc_sbuf_tensor_at(name, [P, *shape], F32R, offset=byte)

        def split(name, off, n):
            return [over(f"{name}{p}", arena_at + 4 * (off + i * n * T), n, T) for i, p in enumerate("hl")]

        wraw = [wr[i // 2][:, 2 * (i % 2):2 * (i % 2) + 2, :] for i in range(4)]
        wh = [over(f"wh{i}", w_at[2 + i // 2] + 4096 * (i % 2), 2, 512) for i in range(4)]
        wl = [over(f"wl{i}", h_at + 4096 * i, 2, 512) for i in range(4)]
        A1, B1, B2 = NH * T, NH * T + 8192, NH * T + 16384
        o_s = split("o", A1, NH)
        h_s = split("h", A1, KD)
        at[0] = B1
        hg_s = split("hg", B1, 4)
        take(8 * T)
        sg = take(4, T)
        hgt = take(4, T)
        sqn = take(KD, T)
        assert at[0] == B2
        braw = [take(PAIRS, 32) for _ in range(2)]
        craw = [take(8, P) for _ in range(2)]
        bbar = [take(PAIRS, 32) for _ in range(2)]
        btmp = take(PAIRS, 32)
        araw = take(3, P)
        ldraw = sb("ldraw", [P, 2])
        prm = take(20, PAIRS)
        at[0] = 0
        BC = take(8, 4, P)
        E1r, E1i, E16r, E16i = (take(PAIRS, 16) for _ in range(4))
        rdec = take(PAIRS)
        gst = take(2, T)
        hst = [take(2, T) for _ in range(2)]
        assert at[0] <= A1
        at[0] = B1
        uT = take(8, T)
        zb = take(8, T)
        yb = take(8, T)
        cgb = take(4, T)
        cvb = take(4, T)
        m_at = at[0]
        szb = take(4, T)
        tabs = [take(2, T) for _ in range(2)]
        p1 = take(2, T)
        p2 = take(2, T)
        bcur = [take(4, P) for _ in range(2)]
        ucur = [take(T) for _ in range(2)]
        yaT = take(KD, T)
        rs = take(T)
        cols = take(7, KD)
        ga1p, sc2p, g1, b1, ag, ab, ga2p = (cols[:, i, :] for i in range(7))
        ptmp = masks[:, 0:4, :].rearrange("p a b -> p (a b)").rearrange("p (a b) -> p a b", a=2)
        yb_s = split("yb", B1 + 24 * T, 8)
        ya_s = split("ya", B1, KD)
        m_s = split("m", m_at, KD)
        yg_s = split("yg", 4096, 8)
        at[0] = 0
        glu = take(8, T)
        gat = take(4, T)
        gbt = take(4, T)
        mt = glu[:, 0:4, :]
        at[0] = A1
        sqo = take(KD, T)
        xo = take(KD, T)
        ostage = [arena[:, i * D:(i + 1) * D] for i in range(2)]

        pg = [ctx.enter_context(nc.psum_tensor(f"pg{i}", [P, 1024], F32)) for i in range(2)]
        pd = [ctx.enter_context(nc.psum_tensor(f"pd{i}", [P, 1024], F32)) for i in range(2)]

        s_vec = sem("s_vec")
        s_x = sem("s_x")
        s_wba = sem("s_wba")
        s_w = [sem(f"s_w{i}") for i in range(4)]
        s_mw = [sem(f"s_mw{i}") for i in range(2)]
        s_unit = sem("s_unit")
        s_cd = sem("s_cd")
        s_zo = sem("s_zo")
        s_cv = sem("s_cv")
        s_acc = sem("s_acc")
        s_pe = sem("s_pe")
        s_v = sem("s_v")
        s_a = sem("s_a")
        s_g = sem("s_g")
        s_cst = sem("s_cst")
        s_p0 = sem("s_p0")
        s_a0 = sem("s_a0")
        s_v0 = sem("s_v0")
        s_vv, s_aa, s_gg = sem("s_vv"), sem("s_aa"), sem("s_gg")
        s_ev = sem("s_ev")
        s_hg = sem("s_hg")
        s_pn = sem("s_pn")
        s_vn = sem("s_vn")
        s_an = sem("s_an")
        s_sg = sem("s_sg")
        s_hc = sem("s_hc")
        s_lc = sem("s_lc")
        s_ck = sem("s_ck")
        s_oh = sem("s_oh")
        s_os = sem("s_os")
        s_hm = sem("s_hm")
        s_dn = sem("s_dn")
        s_raw = sem("s_raw")
        s_pp = sem("s_pp")
        s_ap = sem("s_ap")
        s_vx = sem("s_vx")
        s_vp = sem("s_vp")
        s_uz = sem("s_uz")
        s_cg = sem("s_cg")
        s_vo = sem("s_vo")
        s_tp = sem("s_tp")
        s_bg = sem("s_bg")
        s_za = sem("s_za")
        s_ya = sem("s_ya")
        s_cur = sem("s_cur")
        s_tab = sem("s_tab")
        s_xp = sem("s_xp")
        s_h = sem("s_h")
        s_yp = sem("s_yp")
        s_yt = sem("s_yt")
        s_gate = sem("s_gate")
        s_gel = sem("s_gel")
        s_glu = sem("s_glu")
        s_yg = sem("s_yg")
        s_yl = sem("s_yl")
        s_yah = sem("s_yah")
        s_yal = sem("s_yal")
        s_m = sem("s_m")
        s_gb = sem("s_gb")
        s_ms = sem("s_ms")
        s_x3 = sem("s_x3")
        s_po = sem("s_po")
        s_ao = sem("s_ao")
        s_out = sem("s_out")

        def chain(eng, own):
            n = [0]

            def link(ins):
                n[0] += 1
                ins.then_inc(own, 1)
                eng.wait_ge(own, n[0])

            def restart():
                eng.sem_clear(own)
                n[0] = 0
            return link, restart

        w_in = A["gdn_w_in"][0].rearrange("(k p) n -> p k n", p=P)
        mod_w = A["mod_w"][0].rearrange("(k p) n -> p k n", p=P)
        w_out = A["gdn_w_out"][0].rearrange("(k p) n -> p k n", p=P)

        w_in2 = A["w_in_2"][0].rearrange("(k p) n -> p k n", p=P)
        w_oa = A["w_out_a_2"][0].rearrange("(k p) n -> p k n", p=P)
        w_ob = A["w_out_b_2"][0].rearrange("(k p) n -> p k n", p=P)
        w_glu = A["w_glu_2"][0].rearrange("(k p) n -> p k n", p=P)
        w_o = A["w_o_2"][0].rearrange("(k p) n -> p k n", p=P)
        w_gu = A["ffn_w_gu"][0].rearrange("(k p) n -> p k n", p=P)
        w_down = A["ffn_w_down"][0].rearrange("(k p) n -> p k n", p=P)

        block = ctx.enter_context(nc.Block())

        @block.sync
        def _(sp):
            def mod_load(t):
                k = 4 * (t % 4)
                sp.dma_start(wr[t % 4][:], mod_w[:, k:k + 4, (t // 4) * 512:(t // 4 + 1) * 512]).then_inc(s_w[t % 4], 16)

            with nc.allow_non_contiguous_dma("small vectors"):
                rows = []

                def vrow(col, src):
                    n = src.shape[0]
                    tile, r = col // P, col % P
                    assert r + n <= P
                    rows.append((vstage[r:r + n, tile, :], src))
                one = lambda a: a.rearrange("(r c) -> r c", c=P)
                vrow(V_MODB, one(A["mod_b"][0]))
                vrow(V_C, one(A["c"][0]))
                vrow(V_FG, one(A["final_g_2"]))
                vrow(V_LNG, A["ln_g"][0].rearrange("a (r c) -> (a r) c", c=P))
                vrow(V_LNB, A["ln_b"][0].rearrange("a (r c) -> (a r) c", c=P))
                vrow(V_NG, one(A["norm_g_2"][0]))
                vrow(V_CW2, A["conv_w_2"][0].rearrange("a (r c) -> (a r) c", c=P))
                cw = A["gdn_conv_w"][0].rearrange("a (r c) -> (a r) c", c=P)
                vrow(V_CW, cw[0:P, :])
                vrow(V_CW + P, cw[P:2 * P, :])
                vrow(V_NW, A["gdn_norm_w"])
                vrow(V_BGLU, one(A["b_glu_2"][0]))
                vrow(V_DSK, A["d_skip_2"][0].rearrange("(r a) c -> r (a c)", r=8))
                assert len(rows) == N_VEC
                for dst, src in rows:
                    sp.dma_start(dst, src).then_inc(s_vec, 16)
                for t in range(4):
                    mod_load(t)
                sp.dma_start(xtok, A["x"][0].rearrange("(t p) n -> p t n", p=P)).then_inc(s_x, 16)
                sp.dma_start(wba, w_in[:, :, GB:GB + 64]).then_inc(s_wba, 16)
                sp.dma_start(alog[0:NH, 0:1], A["gdn_a_log"].rearrange("a h -> h a")).then_inc(s_wba, 16)
                sp.dma_start(alog[0:NH, 1:2], A["gdn_dt_bias"].rearrange("a h -> h a")).then_inc(s_wba, 16)

            def batch_loads(g, first=False):
                for t in range(12):
                    if first and t < 4:
                        sp.wait_ge(s_acc, 29 + t)
                    else:
                        sp.wait_ge(s_unit, g * 12 + (t - 3))
                    slot, ks = t % 4, slice(4 * (t % 4), 4 * (t % 4) + 4)
                    if t < 4:
                        sp.dma_start(wr[slot][:, :, 0:256], w_in[:, ks, bass.ds(g * 256 + GQ, 256)]).then_inc(s_w[slot], 16)
                        sp.dma_start(wr[slot][:, :, 256:512], w_in[:, ks, bass.ds(g * 256 + GK, 256)]).then_inc(s_w[slot], 16)
                    else:
                        col = g * 512 + (GV if t < 8 else GZ)
                        sp.dma_start(wr[slot][:], w_in[:, ks, bass.ds(col, 512)]).then_inc(s_w[slot], 16)

            for t in range(4, 32):
                sp.wait_ge(s_acc, t - 3)
                mod_load(t)
            batch_loads(0, first=True)
            with sp.Fori(0, NIT - 1) as j:
                batch_loads(j + 1)
            for t in range(12):
                sp.wait_ge(s_unit, NIT * 12 + (t - 3))
                g, k = t // 6, 4 * (t % 6)
                sp.dma_start(wr[t % 4][:], w_out[:, k:k + 4, g * 512:(g + 1) * 512]).then_inc(s_w[t % 4], 16)
            def load(j, per, c, src):
                if isinstance(j, int) and c < 4:
                    sp.wait_ge(s_unit, U_OUT - 3 + c)
                sp.wait_ge(s_lc, j * per + (c + 1))
                sp.dma_start(wraw[c % 4], src).then_inc(s_w[c % 4], 16)

            def loads(j, per, c, w, first, n, cols=0):
                for t in range(n):
                    src = w[:, 2 * t:2 * t + 2, first:]
                    load(j, per, c + t, src[:, :, bass.ds(cols, 512)])

            def down_loads(j, per, c, k):
                for n in range(4):
                    for t in range(2):
                        load(j, per, c + 2 * n + t, w_down[:, bass.ds(k * 4 + 2 * t, 2), n * 512:(n + 1) * 512])

            for g in range(2):
                loads(0, 0, 4 * g, w_out[:, 24:32, :], 512 * g, 4)
            for g in range(2):
                loads(0, 0, 8 + 16 * g, w_out, 512 * (g + 2), 16)
            loads(0, 0, CK_FF, w_gu, 0, 8)
            loads(0, 0, CK_FF + 8, w_gu, FF, 8)
            with sp.Fori(0, KF // 4 - 1) as j:
                loads(j, 24, CK_FB, w_gu, 512, 8, j * 512)
                down_loads(j, 24, CK_FB + 8, j)
                loads(j, 24, CK_FB + 16, w_gu, FF + 512, 8, j * 512)
            down_loads(0, 0, CK_FD, KF // 4 - 1)
            with sp.Fori(0, 2) as j:
                loads(j, 16, CK_HYB, w_in2, C_U, 8, j * 512)
                loads(j, 16, CK_HYB + 8, w_in2, C_ZB, 8, j * 512)
            with sp.Fori(0, 4) as j:
                for g, col in enumerate((C_V, C_CG, C_BG, C_ZA)):
                    loads(j, 32, CK_MIX + 8 * g, w_in2, col, 8, j * 512)
            loads(0, 0, CK_GA, w_in2, C_GA, 8)
            for i in range(2):
                loads(0, 0, CK_GLU + 4 * i, w_glu, 512 * i, 4)
            for n in range(4):
                c = CK_TAIL + 28 * n
                loads(0, 0, c, w_in2, C_GB + 512 * n, 8)
                loads(0, 0, c + 8, w_oa, 512 * n, 8)
                loads(0, 0, c + 16, w_ob, 512 * n, 4)
                if n < 3:
                    loads(0, 0, c + 20, w_in2, C_GA + 512 * (n + 1), 8)
            for g in range(4):
                loads(0, 0, CK_O + 8 * g, w_o, 512 * g, 8)
            for t in range(TT):
                sp.wait_ge(s_ao, 4 * (t + 1))
                sp.dma_start(out[0, t * P:(t + 1) * P, :], ostage[t]).then_inc(s_out, 16)
            sp.wait_ge(s_out, 16 * TT)

        @block.gpsimd
        def _(pool):
            link, restart = chain(pool, s_gg)

            def mod_loads(base, t0, n):
                for t in range(t0, t0 + n):
                    pool.wait_ge(s_acc, base + (t - 1))
                    k = t % 4
                    pool.dma_start(mw[t % 2], mod_w[:, 4 * k:4 * k + 4, bass.ds(base * 128 + (t // 4) * 512, 512)])\
                        .then_inc(s_mw[t % 2], 16)

            nc.gpsimd.memset(ones[:], 1.0).then_inc(s_cst, 1)
            nc.gpsimd.memset(onesd[:], 1.0 / D).then_inc(s_cst, 1)
            for c, v in enumerate((EPS, LN_EPS, LN_QSCALE, 1.0)):
                nc.gpsimd.memset(cst[:, c:c + 1], v).then_inc(s_cst, 1)
            link(nc.gpsimd.memset(ident[:], 0.0))
            nc.gpsimd.affine_select(out=ident[:], in_=ident[:], compare_op=ALU.not_equal, fill=1.0, base=0,
                                    pattern=[[-1, P]], channel_multiplier=1).then_inc(s_cst, 1)
            link(nc.gpsimd.memset(mneg[:], 0.0))
            nc.gpsimd.affine_select(out=mneg[:], in_=mneg[:], compare_op=ALU.is_ge, fill=BIG, base=0,
                                    pattern=[[1, P]], channel_multiplier=-1).then_inc(s_cst, 1)
            for s, m in [(1, m1t)] + list(msk.items()):
                link(nc.gpsimd.memset(m[:], 0.0))
                nb = P // (2 * s)
                half = m[:].rearrange("p (b two s) -> p b two s", two=2, s=s)
                v = half[:, :, 1, :] if s == 1 else half[:, :, 0, :]
                lo, hi = (0, 0) if s == 1 else (s, 2 * s - 1)
                link(nc.gpsimd.memset(v, 1.0))
                link(nc.gpsimd.affine_select(out=v, in_=v, compare_op=ALU.is_ge, fill=0.0, base=-lo,
                                             pattern=[[-2 * s, nb], [0, s]], channel_multiplier=1))
                nc.gpsimd.affine_select(out=v, in_=v, compare_op=ALU.is_ge, fill=0.0, base=hi,
                                        pattern=[[2 * s, nb], [0, s]], channel_multiplier=-1).then_inc(s_cst, 1)

            def batch(it):
                restart()
                pool.wait_ge(s_a, it * len(AO) + 1)
                nc.gpsimd.tensor_tensor(sqb, qk.rearrange("p a b -> p (a b)"), qk.rearrange("p a b -> p (a b)"),
                                        ALU.mult).then_inc(s_g, 1)
                pool.wait_ge(s_v0, V0["tok"])
                rows = gcT[0:NH].rearrange("p (c t) -> p c t", c=TT).unsqueeze(2).broadcast_to([NH, TT, VH, P])
                pick = ident[0:NH, bass.ds(it * VH, VH)].unsqueeze(1).unsqueeze(3).broadcast_to([NH, TT, VH, P])
                nc.gpsimd.tensor_tensor(rowm[0:NH], rows, pick, ALU.mult).then_inc(s_g, 1)
                mod_loads(it * 8 + 32, 0, 8)

            pool.wait_ge(s_p0, 13)
            gcT = gx[:, 3, :]
            with pool.Fori(0, NIT) as j:
                batch(j)
            restart()
            pool.wait_ge(s_v, NIT * len(VO))
            for m in braw + craw:
                link(nc.gpsimd.memset(m, 0.0))
            with nc.allow_non_contiguous_dma("small parameters"):
                pool.dma_start(araw[0:PAIRS, 0, :], A["a_re_2"][0].rearrange("(r g) p -> r (g p)", g=2)).then_inc(s_raw, 16)
                pool.dma_start(araw[0:PAIRS, 1, :], A["a_im_2"][0].rearrange("(r g) p -> r (g p)", g=2)).then_inc(s_raw, 16)
                pool.dma_start(ldraw[0:PAIRS, :], A["log_dt_2"][0].rearrange("(r g) -> r g", g=2)).then_inc(s_raw, 16)
                for c, nm in enumerate(("re", "im")):
                    for g in range(2):
                        pool.dma_start(braw[c][64 * g:64 * g + 64, :, 16 * g:16 * g + 16],
                                       A[f"b_{nm}_2"][0].rearrange("(r g) p c -> g p r c", g=2)[g]).then_inc(s_raw, 16)
                        for i in range(4):
                            q = 32 * i + 16 * g
                            pool.dma_start(craw[c][q:q + 16, :, 64 * g:64 * g + 64],
                                           A[f"c_{nm}_2"][0].rearrange("(t i g) c p -> i g c t p", i=4, g=2)[i, g])\
                                .then_inc(s_raw, 16)

            def tables(j, q):
                p = bass.ds(j * 8 + q, 1)
                c, s = (tabs[q % 2][:, i, :].rearrange("p (a b) -> p a b", a=16) for i in range(2))
                ta, tb_ = (ptmp[:, i, :].rearrange("p (a b) -> p a b", a=16) for i in range(2))
                big = lambda e: e[:, p, :].squeeze(1).unsqueeze(2).broadcast_to([P, 16, 16])
                small = lambda e: e[:, p, :].squeeze(1).unsqueeze(1).broadcast_to([P, 16, 16])
                tt = nc.gpsimd.tensor_tensor
                pool.wait_ge(s_tab, j * 8 + (q + 1))
                pool.wait_ge(s_h, j * 8 + (q + 1))
                tt(c, big(E16r), small(E1r), ALU.mult)
                link(tt(ta, big(E16i), small(E1i), ALU.mult))
                tt(s, big(E16r), small(E1i), ALU.mult)
                link(tt(tb_, big(E16i), small(E1r), ALU.mult))
                tt(c, c, ta, ALU.subtract)
                tt(s, s, tb_, ALU.add).then_inc(s_tab, 1)

            pool.wait_ge(s_vp, 2)
            pool.wait_ge(s_ap, 6)
            pool.wait_ge(s_uz, 6)
            pool.sem_inc(s_tab, 1)
            with pool.Fori(0, 4) as j:
                restart()
                for q in range(8):
                    if q % 4 == 0:
                        i = q // 4
                        pool.wait_ge(s_yp, j * 8 + (4 * i + 4))
                        pool.wait_ge(s_yt, j * 2 + (i + 1))
                        t = bass.ds(j * 2 + i, 1)
                        nc.gpsimd.tensor_copy(ucur[i], uT[:, t, :].squeeze(1))
                        nc.gpsimd.tensor_copy(bcur[i], BC[:, t].squeeze(1)).then_inc(s_cur, 1)
                    tables(j, q)

        @block.tensor
        def _(pe):
            def tr(dst, src):
                n = src.shape[0]
                return nc.tensor.transpose(dst, src, ident[0:n, 0:n])

            pe.wait_ge(s_cst, N_CST)
            pe.wait_ge(s_vec, 16 * N_VEC)
            for t, n in enumerate(V_ROWS):
                m = tr(pd[0][:, t * P:t * P + n], vstage[0:n, t, :])
            m.then_inc(s_p0, 1)
            pe.wait_ge(s_x, 16)
            for kt in range(KD):
                b = kt // 4
                if kt == 12:
                    pe.wait_ge(s_a0, A0["vec"])
                for t in range(TT):
                    m = tr((pg + pd[::-1])[b][:, (kt % 4) * T + t * P:(kt % 4) * T + (t + 1) * P],
                           xtok[:, t, kt * P:(kt + 1) * P])
                if kt % 4 == 3:
                    m.then_inc(s_p0, 1)
            for ch in range(8):
                pe.wait_ge(s_acc, 4 * (ch + 1))
                if ch == 0:
                    pe.wait_ge(s_a0, A0["x3"])
                for q in range(4):
                    for i, a in enumerate((acc, acc2)):
                        m = nc.tensor.matmul(pd[0][:, 4 * ch + q:4 * ch + q + 1], a[:, ch % 2, q * P:(q + 1) * P],
                                             ones[:, 0:1], start=(i == 0), stop=(i == 1))
                m.then_inc(s_p0, 1)
            pe.wait_ge(s_v0, V0["h"])
            pe.wait_ge(s_wba, 48)
            for w in range(2):
                for k in range(KD):
                    m = nc.tensor.matmul(pd[1][0:NH, w * 512:w * 512 + T], wba[:, k, w * NH:(w + 1) * NH], hT[:, k, :],
                                         start=(k == 0), stop=(k == KD - 1))
            m.then_inc(s_p0, 1)
            pe.wait_ge(s_v0, V0["gc"])
            for n, (row, c) in enumerate(((3, 0), (3, 1), (2, 0), (2, 1), (0, 0))):
                m = tr(pd[0][:, 512 + n * NH:512 + (n + 1) * NH], gx[0:NH, row, c * P:(c + 1) * P])
            m.then_inc(s_p0, 1)

            def unit(slot, pair, kt0, first, last):
                for n in range(4):
                    for k in range(4):
                        yield nc.tensor.matmul(
                            pg[pair][:, n * T:(n + 1) * T], wr[slot][:, k, n * P:(n + 1) * P], hT[:, kt0 + k, :],
                            start=(first and k == 0 and n % 2 == 0), stop=(last and k == 3), skip_group_check=True)

            def gemm(g, base):
                for t in range(12):
                    slot, grp = t % 4, t // 4
                    pe.wait_ge(s_w[slot], g * 64 + (W_MOD + 32 + 16 * grp))
                    if t == 0 and base:
                        pe.wait_ge(s_zo, g)
                    if t == 4 and base:
                        pe.wait_ge(s_cd, g * 2)
                    if t == 8:
                        pe.wait_ge(s_cd, g * 2 + 1)
                    for n, m in enumerate(unit(slot, grp % 2, 4 * slot, slot == 0, slot == 3)):
                        if n == 7:
                            yield
                    m.then_inc(s_unit, 1)
                    yield

            def pdv(i):
                return pd[i][:].rearrange("p (c h t) -> p c h t", c=TT, h=VH)

            def delta(it):
                bp, bv, ba, bg = it * len(PEO), it * len(VO), it * len(AO), it * len(GO)

                def V(name): pe.wait_ge(s_v, bv + VO[name])
                def Ac(name): pe.wait_ge(s_a, ba + AO0 + AO[name])
                pe.wait_ge(s_g, bg + GO["sq"])
                pe.wait_ge(s_v, bv)
                for n in range(2):
                    m = nc.tensor.matmul(pd[0][:, n * 512:(n + 1) * 512], ones[:], sqb[:, n * 512:(n + 1) * 512],
                                         start=True, stop=True)
                m.then_inc(s_pe, 1)
                pe.wait_ge(s_g, bg + GO["rowm"])
                for n in range(2):
                    m = nc.tensor.matmul(pd[1][:, n * 512:(n + 1) * 512], ones[0:NH, :],
                                         rowm[0:NH, n].rearrange("p a b -> p (a b)"), start=True, stop=True)
                m.then_inc(s_pe, 1)
                yield
                Ac("rn")
                for c in range(TT):
                    for h in range(VH):
                        m = tr(pdv(0)[:, c, h], vT[:, h, c * P:(c + 1) * P])
                m.then_inc(s_pe, 1)
                yield
                V("qkn")
                Ac("vtok")
                for w in range(2):
                    for c in range(TT):
                        for h in range(2):
                            m = nc.tensor.matmul(pd[0][:, w * 512 + (c * 2 + h) * P:w * 512 + (c * 2 + h + 1) * P],
                                                 qk[:, 2 + h, c * P:(c + 1) * P],
                                                 qk[:, (2 if w == 0 else 0) + h, c * P:(c + 1) * P],
                                                 start=True, stop=True)
                m.then_inc(s_pe, 1)
                V("dt")
                for h in range(2):
                    m = tr(pd[1][:, h * P:(h + 1) * P], qk[:, 2 + h, 0:P])
                m.then_inc(s_pe, 1)
                yield
                V("u2")
                Ac("kg")
                for n in range(8):
                    m = tr(pd[1][:, n * P:(n + 1) * P], Ub[:, n, :])
                m.then_inc(s_pe, 1)
                yield
                par = 0

                def x_step(s):
                    for n in range(8):
                        m = nc.tensor.matmul(pd[par][:, n * P:(n + 1) * P], lTb[:, n, :], Tb[:, n, :],
                                             start=True, stop=True)
                    m.then_inc(s_pe, 1)
                V("at")
                Ac("t2")
                x_step(2)
                yield
                for s in LEVELS:
                    V(f"x{s}")
                    if s > 2:
                        Ac(f"u{s // 2}")
                    par ^= 1
                    for n in range(8):
                        m = nc.tensor.matmul(pd[par][:, n * P:(n + 1) * P], Ub[:, n, :], Xb[:, n, :],
                                             start=True, stop=True)
                    m.then_inc(s_pe, 1)
                    yield
                    V(f"t{s}")
                    par ^= 1
                    for n in range(8):
                        m = tr(pd[par][:, n * P:(n + 1) * P], Tb[:, n, :])
                    m.then_inc(s_pe, 1)
                    par ^= 1
                    x_step(2 * s)
                    yield
                V("x64")
                Ac("u32")
                par ^= 1
                for n in range(8):
                    m = nc.tensor.matmul(pd[par][:, n * P:(n + 1) * P], Xb[:, n, :], Ub[:, n, :],
                                         start=True, stop=True)
                m.then_inc(s_pe, 1)
                assert par == 0
                yield
                V("u64")
                for h in range(VH):
                    m = nc.tensor.matmul(pd[1][:, h * P:(h + 1) * P], Ub[:, h, :], vtok[:, h, :], start=True, stop=True)
                m.then_inc(s_pe, 1)
                yield
                Ac("v0")
                for h in range(VH):
                    m = nc.tensor.matmul(pd[0][:, h * P:(h + 1) * P], kg0[:, h, :], vn0[:, h, :], start=True, stop=True)
                m.then_inc(s_pe, 1)
                for h in range(VH):
                    m = nc.tensor.matmul(pd[0][:, 512 + h * P:512 + (h + 1) * P], aTb[:, h, :], vn0[:, h, :],
                                         start=True, stop=True)
                m.then_inc(s_pe, 1)
                yield
                Ac("s")
                for h in range(VH):
                    m = nc.tensor.matmul(pd[1][:, h * P:(h + 1) * P], qk[:, 2 + h // 2, P:T], Sb[:, h, :],
                                         start=True, stop=True)
                m.then_inc(s_pe, 1)
                for h in range(VH):
                    m = nc.tensor.matmul(pd[1][:, 512 + h * P:512 + (h + 1) * P], qk[:, h // 2, P:T], Sb[:, h, :],
                                         start=True, stop=True)
                m.then_inc(s_pe, 1)
                yield
                V("rhs1")
                for h in range(VH):
                    m = nc.tensor.matmul(pd[0][:, h * P:(h + 1) * P], Ub[:, VH + h, :], rhs1[:, h, :],
                                         start=True, stop=True)
                m.then_inc(s_pe, 1)
                yield
                Ac("v1")
                Ac("qs")
                for h in range(VH):
                    m = nc.tensor.matmul(pd[1][:, h * P:(h + 1) * P], aTb[:, VH + h, :], vn1[:, h, :],
                                         start=True, stop=True)
                m.then_inc(s_pe, 1)
                yield
                V("on")
                for c in range(TT):
                    for h in range(VH):
                        m = tr(pdv(0)[:, c, h], ob[:, c * VH + h, :])
                m.then_inc(s_pe, 1)
                yield
                pe.wait_ge(s_acc, it * 8 + 40)
                for q in range(8):
                    m = nc.tensor.matmul(pd[1][:, q:q + 1], acc[:, q // 4, (q % 4) * P:(q % 4 + 1) * P],
                                         ones[:, 0:1], start=True, stop=True)
                m.then_inc(s_pe, 1)
                yield

            for _ in gemm(0, False):
                pass
            with pe.Fori(0, NIT - 1) as j:
                steps = delta(j)
                for part, _ in enumerate(gemm(j + 1, True)):
                    if part >= PARTS_FIRST:
                        next(steps, None)
                for _ in steps:
                    pass
            def early_out():
                for t in range(12):
                    slot, g, k0 = t % 4, t // 6, 4 * (t % 6)
                    pe.wait_ge(s_w[slot], W_MOD + 64 * NIT + 16 * (t // 4 + 1))
                    if t == 0:
                        pe.wait_ge(s_v, 6 * len(VO))
                        pe.wait_ge(s_zo, NIT)
                    if t == 6:
                        pe.wait_ge(s_cd, NIT * 2)
                    for n in range(4):
                        for k in range(4):
                            m = nc.tensor.matmul(pg[g][:, n * T:(n + 1) * T], wr[slot][:, k, n * P:(n + 1) * P],
                                                 oT[:, k0 + k, :], start=(k0 == 0 and k == 0 and n % 2 == 0),
                                                 stop=False, skip_group_check=True)
                        if n == 1:
                            yield
                    m.then_inc(s_unit, 1)
                    yield

            steps = delta(NIT - 1)
            for part, _ in enumerate(early_out()):
                if part >= PARTS_FIRST:
                    next(steps, None)
            for _ in steps:
                pass
            pe.sem_inc(s_ck, 4)

            def chunk(j, per, c, bank, act, k0, first, last):
                pe.wait_ge(s_lc, j * per + (c + 5))
                s = c % 4
                for n in range(4):
                    for k in range(2):
                        for i, (w, x) in enumerate(((wh, 0), (wh, 1), (wl, 0))):
                            m = nc.tensor.matmul(bank[:, n * T:(n + 1) * T], w[s][:, k, n * P:(n + 1) * P],
                                                 act[x][:, k0 + k, :], skip_group_check=True,
                                                 start=(first and k == 0 and i == 0 and n % 2 == 0),
                                                 stop=(last and k == 1 and i == 2))
                m.then_inc(s_ck, 1)

            def group(j, per, c, bank, act, n, need=None, k0=0):
                for t in range(n):
                    if need:
                        need(t)
                    chunk(j, per, c + t, bank, act, k0 + 2 * t, t == 0, t == n - 1)

            for t in range(CK_FF):
                g, k, last = out_chunk(t)
                if t < 8:
                    pe.wait_ge(s_os, o_ready(2 * k))
                elif t < 24:
                    if t == 8:
                        pe.wait_ge(s_ev, 1)
                    pe.wait_ge(s_os, o_ready(2 * k))
                elif t == 24:
                    pe.wait_ge(s_ev, 2)
                chunk(0, 0, t, pg[g % 2], o_s, 2 * k, g >= 2 and k == 0, last)
                if t == 15:
                    pe.wait_ge(s_raw, 16 * N_RAW)
                    pe.wait_ge(s_vx, 1)
                    for c in range(3):
                        m = tr(pd[0][:, c * PAIRS:(c + 1) * PAIRS], araw[0:PAIRS, c, :])
                    m.then_inc(s_pp, 1)
                    for c in range(8):
                        m = tr(pd[1][:, c * P:(c + 1) * P], craw[1][:, c, :])
                    m.then_inc(s_pp, 1)
                if t == 19:
                    pe.wait_ge(s_ap, 1)
                    for c in range(8):
                        m = tr(pd[0][:, c * P:(c + 1) * P], craw[0][:, c, :])
                    m.then_inc(s_pp, 1)
                if t == 38:
                    pe.wait_ge(s_vp, 1)
                    pe.wait_ge(s_ap, 3)
                    for i in range(2):
                        for c in range(8):
                            m = tr(pd[i][:, c * P:(c + 1) * P],
                                   bbar[i][:, 4 * c:4 * c + 4, :].rearrange("p a b -> p (a b)"))
                    m.then_inc(s_pp, 1)

            def mean(bank, ready, src):
                for c in range(4):
                    pe.wait_ge(*ready(c))
                    for k in range(4 * c, 4 * c + 4):
                        m = nc.tensor.matmul(bank[:, 0:T], onesd[:], src[:, k, :], start=(k == 0), stop=(k == KD - 1))
                m.then_inc(s_pn, 1)

            pe.wait_ge(s_ap, 6)
            mean(pd[0], lambda c: (s_ev, c + 1), xT)
            mean(pd[1], lambda c: (s_an, AN["sqa"] + c), sqn)

            def down(j, per, c, it):
                pe.wait_ge(s_hg, it + 1)
                for n in range(4):
                    pe.wait_ge(s_dn, it * 4 + (n + 1))
                    group(j, per, c + 2 * n, pd[n % 2], hg_s, 2)
            group(0, 0, CK_FF, pg[0], h_s, 8, lambda t: pe.wait_ge(s_vn, VN["ha"] + t // 2))
            group(0, 0, CK_FF + 8, pg[1], h_s, 8)
            with pe.Fori(0, KF // 4 - 1) as j:
                pe.wait_ge(s_sg, j + 1)
                group(j, 24, CK_FB, pg[0], h_s, 8)
                down(j, 24, CK_FB + 8, j)
                pe.wait_ge(s_hm, j + 1)
                group(j, 24, CK_FB + 16, pg[1], h_s, 8)
            down(0, 0, CK_FD, KF // 4 - 1)
            mean(pg[0], lambda c: (s_dn, 2 + KF - 4 + c + 1), xT)
            mean(pg[1], lambda c: (s_an, AN["sqb"] + c), sqn)
            mean(pd[0], lambda c: (s_an, AN["sqc"] + c), sqn)

            with pe.Fori(0, 2) as j:
                for i in range(2):
                    pe.wait_ge(s_uz, j * 2 + (i + 1))
                    group(j, 16, CK_HYB + 8 * i, pg[i], h_s, 8, lambda t: pe.wait_ge(s_vn, VN["hc"] + t // 2))

            def state_in(j, q):
                pe.wait_ge(s_cur, j * 2 + (q // 4 + 1))
                pe.wait_ge(s_h, j * 8 + (q + 1))
                r = slice(32 * (q % 4), 32 * (q % 4) + 32)
                for c in range(2):
                    m = nc.tensor.matmul(pd[0][:, (q % 2) * 512 + c * T:(q % 2) * 512 + (c + 1) * T],
                                         bcur[q // 4][r, c, :], ucur[q // 4][r, :], start=True, stop=True)
                m.then_inc(s_xp, 1)

            def state_out(j, q):
                pe.wait_ge(s_h, j * 8 + (q + 3))
                if q % 4 == 0:
                    pe.wait_ge(s_yt, j * 2 + (q // 4 + 1))
                r = slice(32 * (q % 4), 32 * (q % 4) + 32)
                for c in range(2):
                    m = nc.tensor.matmul(pd[1][r, (q // 4) * 512:(q // 4) * 512 + T], bcur[q // 4][:, 2 + c, r],
                                         hst[q % 2][:, c, :], start=(c == 0), stop=(c == 1))
                m.then_inc(s_yp, 1)

            pe.sem_inc(s_yp, 8)
            pe.wait_ge(s_uz, 6)
            with pe.Fori(0, 4) as j:
                for t in range(32):
                    if t == 0:
                        pe.wait_ge(s_bg, j + 1)
                    if t == 8:
                        pe.wait_ge(s_za, j + 1)
                    if t == 16:
                        pe.wait_ge(s_cg, j + 1)
                    if t == 24:
                        pe.wait_ge(s_vo, j + 1)
                    chunk(j, 32, CK_MIX + t, pg[(t // 8) % 2], h_s, 2 * (t % 8), t % 8 == 0, t % 8 == 7)
                    if t % 4 == 0:
                        state_in(j, t // 4)
                    if t % 4 == 3:
                        state_out(j, t // 4)
            pe.wait_ge(s_bg, 5)
            group(0, 0, CK_GA, pg[0], h_s, 8)
            pe.wait_ge(s_za, 5)
            pe.wait_ge(s_yl, 1)
            for i, bank in enumerate((pg[1], pd[1])):
                group(0, 0, CK_GLU + 4 * i, bank, yb_s, 4)

            def tail(j, per, c, n, last=False, first=False):
                pe.wait_ge(s_gb, n + 1)
                group(j, per, c, pd[1], h_s, 8)
                pe.wait_ge(s_m, n + 1)
                group(j, per, c + 8, pd[0], ya_s, 8, (lambda t: pe.wait_ge(s_yal, t // 2 + 1)) if first else None)
                pe.wait_ge(s_ms, n + 1)
                if first:
                    pe.wait_ge(s_yg, 2)
                group(j, per, c + 16, pg[1], yg_s, 4)
                if not last:
                    pe.wait_ge(s_gate, n + 1)
                    group(j, per, c + 20, pg[0], h_s, 8)
            pe.wait_ge(s_glu, 2)
            tail(0, 0, CK_TAIL, 0, first=True)
            with pe.Fori(1, 3) as j:
                tail(j, 28, CK_TAIL, j)
            tail(0, 0, CK_LAST, 3, last=True)
            pe.wait_ge(s_gb, 5)
            pe.wait_ge(s_m, 5)
            for g in range(4):
                if g >= 2:
                    pe.wait_ge(s_x3, g - 1)
                group(0, 0, CK_O + 8 * g, pd[g % 2], m_s, 8,
                      (lambda t: pe.wait_ge(s_ms, t // 2 + 2)) if g == 0 else None)
            mean(pd[0], lambda c: (s_an, AN["sqd"] + c), sqo)
            for t in range(TT):
                for b in range(4):
                    n = t * 4 + b
                    pe.wait_ge(s_vn, VN["xo"] + b)
                    if n >= 2:
                        pe.wait_ge(s_ao, n - 1)
                    for k in range(4):
                        m = tr(pg[n % 2][:, k * P:(k + 1) * P], xo[:, 4 * b + k, t * P:(t + 1) * P])
                    m.then_inc(s_po, 1)

        @block.scalar
        def _(act):
            link, restart = chain(act, s_aa)
            a = nc.scalar.activation
            act.wait_ge(s_p0, 1)
            for t in range(2):
                a(vc[:, t * 320:(t + 1) * 320], pd[0][:, t * 320:(t + 1) * 320], ACT.Copy).then_inc(s_a0, 1) if t == 0 else \
                    a(vc[:, 320:V_DSK + 8], pd[0][:, 320:V_DSK + 8], ACT.Copy).then_inc(s_a0, 1)
            act.wait_ge(s_a0, 2)
            a(condt[:], vc[:, V_C:V_C + KD], ACT.Silu).then_inc(s_a0, 1)
            for b in range(4):
                act.wait_ge(s_p0, 2 + b)
                a(xT[:, 4 * b:4 * b + 4, :].rearrange("p a b -> p (a b)"), (pg + pd[::-1])[b][:], ACT.Copy).then_inc(s_a0, 1)
            act.wait_ge(s_p0, 14)
            a(gx[0:NH, 2, :], pd[1][0:NH, 0:T], ACT.Sigmoid).then_inc(s_a0, 1)
            link(a(aT[0:NH], pd[1][0:NH, 512:512 + T], ACT.Identity, bias=alog[0:NH, 1:2]))
            link(a(bT[0:NH], aT[0:NH], ACT.Abs))
            nc.scalar.preload_act_table_set("natural_log_exp_and_others")
            link(a(bT[0:NH], bT[0:NH], ACT.Exp, scale=-1.0))
            a(bT[0:NH], bT[0:NH], ACT.Ln, bias=cst[0:NH, 3:4]).then_inc(s_a0, 1)
            a(alog[0:NH, 2:3], alog[0:NH, 0:1], ACT.Exp).then_inc(s_a0, 1)
            act.wait_ge(s_p0, 15)
            act.wait_ge(s_v0, V0["gc"])
            a(tk[:, 0:4, :].rearrange("p a b -> p (a b)"), pd[0][:, 512:512 + 4 * NH], ACT.Copy).then_inc(s_a0, 1)
            a(tk[:, 4, :], pd[0][:, 512 + NH:512 + 2 * NH], ACT.Exp).then_inc(s_a0, 1)
            a(tk[:, 6, :], pd[0][:, 512 + 4 * NH:512 + 5 * NH], ACT.Exp).then_inc(s_a0, 1)

            def tap(g, grp):
                act.wait_ge(s_unit, g * 12 + 4 * (grp + 1))
                for n in range(4):
                    a(pend[:, grp * 4 + n, :], pg[grp][:, n * T:(n + 1) * T], ACT.Copy,
                      scale=cwc[:, 3, grp * 4 + n:grp * 4 + n + 1]).then_inc(s_cv, 1)

            def z_out(g):
                act.wait_ge(s_unit, g * 12 + 12)
                a(zpend.rearrange("p a b -> p (a b)"), pg[0][:], ACT.Copy).then_inc(s_zo, 1)

            def silus(g):
                act.wait_ge(s_cd, g * 2 + 2)
                link(a(qk.rearrange("p a b -> p (a b)"), pend[:, 0:4, :].rearrange("p a b -> p (a b)"), ACT.Silu))
                a(vT.rearrange("p a b -> p (a b)"), pend[:, 4:8, :].rearrange("p a b -> p (a b)"), ACT.Silu).then_inc(s_a, 1)

            def silu_z(g):
                act.wait_ge(s_zo, g + 1)
                a(zT.rearrange("p a b -> p (a b)"), zpend.rearrange("p a b -> p (a b)"), ACT.Silu).then_inc(s_a, 1)

            def delta(it):
                bp, bv = it * len(PEO), it * len(VO)
                def PEw(name): act.wait_ge(s_pe, bp + PEO[name])
                def V(name): act.wait_ge(s_v, bv + VO[name])
                restart()
                nc.scalar.preload_act_table_set("natural_log_exp_and_others")
                PEw("ssq")
                link(a(rnb, pd[0][:], ACT.Ln, bias=cst[:, 0:1]))
                link(a(rnb[:, 0:512], rnb[:, 0:512], ACT.Exp, scale=-0.5, bias=cst[:, 2:3]))
                a(rnb[:, 512:1024], rnb[:, 512:1024], ACT.Exp, scale=-0.5).then_inc(s_a, 1)
                V("dt")
                a(dTb.rearrange("p a b -> p (a b)"), dTb.rearrange("p a b -> p (a b)"), ACT.Exp).then_inc(s_a, 1)
                PEw("vtok")
                a(vtok.rearrange("p a b -> p (a b)"), pd[0][:], ACT.Copy).then_inc(s_a, 1)
                yield
                PEw("ktok")
                for h in range(VH):
                    m = a(kg0[:, h, :], pd[1][:, (h // 2) * P:(h // 2 + 1) * P], ACT.Copy, scale=tkc[:, 6, h:h + 1])
                m.then_inc(s_a, 1)
                yield
                PEw("t2")
                a(Tb.rearrange("p a b -> p (a b)"), pd[1][:], ACT.Copy).then_inc(s_a, 1)
                yield
                par = 0
                for s in LEVELS:
                    PEw(f"u{s}")
                    a(Ub.rearrange("p a b -> p (a b)"), pd[par][:], ACT.Copy).then_inc(s_a, 1)
                    par ^= 1
                    yield
                PEw("v0")
                for h in range(VH):
                    m = a(vn0[:, h, :], pd[1][:, h * P:(h + 1) * P], ACT.Copy, scale=tkc[:, 2, h:h + 1])
                m.then_inc(s_a, 1)
                yield
                PEw("s")
                a(Sb.rearrange("p a b -> p (a b)"), pd[0][:, 0:512], ACT.Copy).then_inc(s_a, 1)
                yield
                PEw("qs")
                for h in range(VH):
                    m = a(ob[:, VH + h, :], pd[1][:, 512 + h * P:512 + (h + 1) * P], ACT.Copy, scale=tkc[:, 4, h:h + 1])
                m.then_inc(s_a, 1)
                PEw("v1")
                for h in range(VH):
                    m = a(vn1[:, h, :], pd[0][:, h * P:(h + 1) * P], ACT.Copy, scale=tkc[:, 3, h:h + 1])
                m.then_inc(s_a, 1)
                yield
                V("o1")
                for n in range(8):
                    link(a(Xb[:, n, :], ob[:, n, :], ACT.Square, accum_out=ssq[:, n:n + 1]))
                link(a(rstd, ssq, ACT.Ln, scale=1.0 / P, bias=cst[:, 0:1]))
                a(rstd, rstd, ACT.Exp, scale=-0.5).then_inc(s_a, 1)
                yield

            act.wait_ge(s_v0, V0["cw"])
            for grp in range(2):
                tap(0, grp)
            z_out(0)
            silus(0)
            silu_z(0)
            with act.Fori(0, NIT - 1) as j:
                steps = delta(j)
                for t in range(9):
                    next(steps)
                    if t == 4:
                        tap(j + 1, 0)
                    if t == 7:
                        tap(j + 1, 1)
                for _ in steps:
                    pass
                z_out(j + 1)
                silus(j + 1)
                act.wait_ge(s_v, j * len(VO) + VO["og"])
                silu_z(j + 1)
            fl = lambda x: x.rearrange("p a b -> p (a b)")

            def high(j, per, c):
                act.wait_ge(s_w[c % 4], j * (4 * per) + (W_GDN + 16 * (c // 4 + 1)))
                act.wait_ge(s_ck, j * per + (c + 1))
                a(wh[c % 4][:], wraw[c % 4], ACT.Copy).then_inc(s_hc, 1)

            def stream(j, per, c, n, events={}):
                for t in range(n):
                    if not (isinstance(j, int) and c + t + AHEAD >= CK_END):
                        high(j, per, c + t + AHEAD)
                    if t in events:
                        events[t]()

            def used(j, per, c):
                act.wait_ge(s_ck, j * per + (c + 5))

            for _ in delta(NIT - 1):
                pass
            act.wait_ge(s_unit, U_OUT)
            for c in range(AHEAD):
                high(0, 0, c)
            act.wait_ge(s_v, NIT * len(VO))

            def o_high(i):
                c = O_ORDER[i]
                a(fl(o_s[0][:, 4 * c:4 * c + 4, :]), fl(oT[:, 4 * c:4 * c + 4, :]), ACT.Copy).then_inc(s_oh, 1)
            o_high(0)
            o_high(1)

            def prep0():
                act.wait_ge(s_os, 8)
                act.wait_ge(s_pp, 1)
                a(fl(prm[:, 0:3, :]), pd[0][:, 0:3 * PAIRS], ACT.Copy).then_inc(s_ap, 1)
                act.wait_ge(s_pp, 2)
                a(BC[:, :, 3, :], pd[1][:].rearrange("p (t s) -> p t s", s=P), ACT.Copy, scale=-1.0).then_inc(s_ap, 1)

            def prep1():
                act.wait_ge(s_pp, 3)
                a(BC[:, :, 2, :], pd[0][:].rearrange("p (t s) -> p t s", s=P), ACT.Copy).then_inc(s_ap, 1)

            def prep2():
                act.wait_ge(s_vx, 2)
                a(prm[:, 8, :], prm[:, 7, :], ACT.Sin)
                a(prm[:, 9, :], prm[:, 7, :], ACT.Sin, scale=0.5).then_inc(s_ap, 1)

            def prep3():
                act.wait_ge(s_pp, 4)
                for c in range(2):
                    a(BC[:, :, c, :], pd[c][:].rearrange("p (t s) -> p t s", s=P), ACT.Copy).then_inc(s_ap, 1)
            stream(0, 0, 0, CK_FF, {**{t: (lambda t=t: o_high(t // 2 + 2)) for t in range(0, 12, 2)},
                                    15: prep0, 19: prep1, 24: prep2, 38: prep3})

            def squares(ready, dst=sqn):
                for c in range(4):
                    act.wait_ge(*ready(c))
                    a(fl(dst[:, 4 * c:4 * c + 4, :]), fl(xT[:, 4 * c:4 * c + 4, :]), ACT.Square).then_inc(s_an, 1)

            def inv_root(bank, n, eps):
                act.wait_ge(s_pn, n)
                restart()
                link(a(rs, bank[:, 0:T], ACT.Ln, bias=cst[:, eps:eps + 1]))
                a(rs, rs, ACT.Exp, scale=-0.5).then_inc(s_an, 1)

            def affine(g, b, ready):
                for c in range(4):
                    act.wait_ge(*ready(c))
                    for k in range(4 * c, 4 * c + 4):
                        m = a(xT[:, k, :], xT[:, k, :], ACT.Identity, scale=g[:, k:k + 1], bias=b[:, k:k + 1])
                    m.then_inc(s_an, 1)

            squares(lambda c: (s_vn, VN["da"] + c))
            inv_root(pd[1], 2, 1)
            affine(ag, ab, lambda c: (s_vn, VN["ha"] + c))

            def gates(j, per, c, it):
                used(j, per, c)
                if not isinstance(it, int):
                    act.wait_ge(s_hm, it)
                a(fl(sg), pg[0][:], ACT.Silu).then_inc(s_sg, 1)
            stream(0, 0, CK_FF, 16, {7: lambda: gates(0, 0, CK_FF + 7, 0)})
            with act.Fori(0, KF // 4 - 1) as j:
                stream(j, 24, CK_FB, 24, {7: lambda: gates(j, 24, CK_FB + 7, j + 1)})
            stream(0, 0, CK_FD, 8)
            nc.scalar.preload_act_table_set("natural_log_exp_and_others")
            squares(lambda c: (s_vn, VN["db"] + c))
            inv_root(pg[1], 4, 1)
            affine(vc[:, V_LNG + KD:V_LNG + 2 * KD], vc[:, V_LNB + KD:V_LNB + 2 * KD], lambda c: (s_vn, VN["nb"] + c))
            squares(lambda c: (s_an, AN["x2"] - 3 + c))
            inv_root(pd[0], 5, 0)

            for sem in (s_uz, s_uz, s_za, s_gb):
                act.sem_inc(sem, 1)

            def out_u(j):
                used(j, 16, CK_HYB + 7)
                a(fl(uT[:, bass.ds(j * 4, 4), :]), pg[0][:], ACT.Copy).then_inc(s_uz, 1)

            def out_zb(j):
                used(j, 16, CK_HYB + 15)
                a(fl(zb[:, bass.ds(j * 4, 4), :]), pg[1][:], ACT.Silu).then_inc(s_uz, 1)
            with act.Fori(0, 2) as j:
                stream(j, 16, CK_HYB, 16, {7: lambda: out_u(j), 15: lambda: out_zb(j)})

            def out_v(j):
                used(j, 32, CK_MIX + 7)
                act.wait_ge(s_bg, j + 1)
                a(fl(cgb), pg[0][:], ACT.Copy).then_inc(s_cg, 1)

            def last_tap(j):
                act.wait_ge(s_vo, j + 1)
                act.wait_ge(s_ya, j + 1)
                for n in range(4):
                    col = bass.ds(j * 4 + (V_CW2 + 2 * KD + n), 1)
                    m = a(cvb[:, n, :], cgb[:, n, :], ACT.Copy, scale=vc[:, col])
                m.then_inc(s_tp, 1)

            def out_za(j):
                used(j, 32, CK_MIX + 31)
                a(fl(szb), pg[1][:], ACT.Silu).then_inc(s_za, 1)
            with act.Fori(0, 4) as j:
                stream(j, 32, CK_MIX, 32, {7: lambda: out_v(j), 16: lambda: last_tap(j), 31: lambda: out_za(j)})

            def gelu():
                act.wait_ge(s_yt, 10)
                a(fl(yb), fl(yb), ACT.Gelu_apprx_tanh).then_inc(s_gel, 1)

            def out_ga(j, per, c):
                used(j, per, c)
                if not isinstance(j, int):
                    act.wait_ge(s_m, j + 2)
                a(fl(gat), pg[0][:], ACT.Sigmoid).then_inc(s_gate, 1)

            def out_gb(j, per, c, n):
                used(j, per, c)
                act.wait_ge(s_ms, n + 1)
                a(fl(gbt), pd[1][:], ACT.Sigmoid).then_inc(s_gb, 1)

            def out_glu(i):
                used(0, 0, CK_GLU + 4 * i + 3)
                for n in range(4):
                    k = 4 * i + n
                    m = a(glu[:, k, :], (pg[1], pd[1])[i][:, n * T:(n + 1) * T], ACT.Sigmoid,
                          bias=vc[:, V_BGLU + k:V_BGLU + k + 1])
                m.then_inc(s_glu, 1)

            def ya_high(c):
                act.wait_ge(s_yg, 2)
                a(fl(ya_s[0][:, 4 * c:4 * c + 4, :]), fl(yaT[:, 4 * c:4 * c + 4, :]), ACT.Copy).then_inc(s_yah, 1)
            stream(0, 0, CK_GA, 8, {0: gelu, 7: lambda: out_ga(0, 0, CK_GA + 7)})
            stream(0, 0, CK_GLU, 8, {3: lambda: out_glu(0), 7: lambda: out_glu(1)})
            stream(0, 0, CK_TAIL, 28, {**{t: (lambda t=t: ya_high(t)) for t in range(4)},
                                       7: lambda: out_gb(0, 0, CK_TAIL + 7, 0),
                                       27: lambda: (act.wait_ge(s_m, 2), out_ga(0, 0, CK_TAIL + 27))})
            with act.Fori(1, 3) as j:
                stream(j, 28, CK_TAIL, 28, {7: lambda: out_gb(j, 28, CK_TAIL + 7, j),
                                            27: lambda: out_ga(j, 28, CK_TAIL + 27)})
            stream(0, 0, CK_LAST, 20, {7: lambda: out_gb(0, 0, CK_LAST + 7, 3)})
            stream(0, 0, CK_O, 32)
            nc.scalar.preload_act_table_set("natural_log_exp_and_others")
            squares(lambda c: (s_x3, c + 1), sqo)
            inv_root(pd[0], 6, 0)
            for n in range(8):
                act.wait_ge(s_po, n + 1)
                a(ostage[n // 4][:, (n % 4) * 512:(n % 4 + 1) * 512], pg[n % 2][:, 0:512], ACT.Copy).then_inc(s_ao, 1)

        @block.vector
        def _(dve):
            v = nc.vector
            link, restart = chain(dve, s_vv)
            stt = v.scalar_tensor_tensor

            def mod_first(ch):
                for i in range(16):
                    t, k = 4 * ch + i // 4, i % 4
                    if k == 0:
                        dve.wait_ge(s_w[t % 4], 16 * (t // 4 + 1))
                    if i >= 2 and k != 1:
                        dve.wait_ge(s_vv, 3 * t + k - 1 if k >= 2 else 3 * t)
                    if i >= 2 and k == 1:
                        dve.wait_ge(s_acc, t)
                    dst = (acc, acc2)[i % 2][:, ch % 2, :]
                    scalar = condt[:, i:i + 1]
                    if i < 2:
                        m = v.tensor_scalar(dst, wr[t % 4][:, k, :], scalar, None, ALU.mult)
                    else:
                        m = stt(out=dst, in0=wr[t % 4][:, k, :], scalar=scalar, in1=dst, op0=ALU.mult, op1=ALU.add)
                    m.then_inc(s_acc if k == 3 else s_vv, 1)

            def mod_units(base, t0, n):
                for t in range(t0, t0 + n):
                    dve.wait_ge(s_mw[t % 2], base * 8 + (16 * (t // 2 + 1) - 8 * 32))
                    for k in range(4):
                        kk = (t % 4) * 4 + k
                        dst = acc[:, (t // 4) % 2, :]
                        if kk == 0:
                            m = v.tensor_scalar(dst, mw[t % 2][:, k, :], condt[:, kk:kk + 1], None, ALU.mult)
                        else:
                            m = stt(out=dst, in0=mw[t % 2][:, k, :], scalar=condt[:, kk:kk + 1], in1=dst,
                                    op0=ALU.mult, op1=ALU.add)
                        if k < 3:
                            link(m)
                    m.then_inc(s_acc, 1)
                    dve.wait_ge(s_acc, base + t + 1)

            dve.wait_ge(s_a0, A0["cond"])
            for ch in range(8):
                if ch >= 2:
                    dve.wait_ge(s_p0, 6 + ch - 1)
                mod_first(ch)
            dve.wait_ge(s_vv, 96)
            restart()
            dve.wait_ge(s_p0, 13)
            dve.wait_ge(s_a0, A0["vec"])
            link(v.tensor_tensor(modt[:, 0:32], pd[0][:, 0:32], vc[:, V_MODB:V_MODB + 32], ALU.add))
            link(v.tensor_scalar(sc1p[:], modt[:, KD:2 * KD], 1.0, None, ALU.add))
            for k in range(KD):
                m = v.tensor_scalar(hT[:, k, :], xT[:, k, :], sc1p[:, k:k + 1], modt[:, k:k + 1], ALU.mult, ALU.add)
            m.then_inc(s_v0, 1)
            cwv = vc[:, V_CW:V_CW + 256].rearrange("p (a t) -> p a t", a=4)

            def taps(g):
                link(v.tensor_copy(cwc[:, :, 0:2], cwv[:, :, bass.ds(g * 2, 2)]))
                link(v.tensor_copy(cwc[:, :, 2:4], cwv[:, :, bass.ds(g * 2 + 16, 2)]))
                return v.tensor_copy(cwc[:, :, 4:8], cwv[:, :, bass.ds(g * 4 + 32, 4)])
            taps(0).then_inc(s_v0, 1)
            dve.wait_ge(s_a0, A0["sp"])
            gxv = lambda r: gx[0:NH, r, :]
            link(stt(out=gxv(1), in0=aT[0:NH], scalar=0.0, in1=bT[0:NH], op0=ALU.max, op1=ALU.add))
            link(v.tensor_scalar(gxv(1), gxv(1), alog[0:NH, 2:3], -1.0, ALU.mult, ALU.mult))
            link(v.memset(gxv(0), 1.0))
            for c in range(TT):
                link(v.tensor_tensor_scan(gx[0:NH, 3, c * P:(c + 1) * P], gx[0:NH, 0, c * P:(c + 1) * P],
                                          gx[0:NH, 1, c * P:(c + 1) * P], 0.0, ALU.mult, ALU.add))
            v.tensor_scalar(gx[0:NH, 0, 0:P], gx[0:NH, 3, 0:P], -1.0, gx[0:NH, 3, P - 1:P], ALU.mult, ALU.add)\
                .then_inc(s_v0, 1)
            dve.wait_ge(s_a0, A0["tok"])
            v.tensor_scalar(tk[:, 5, :], tk[:, 4, :], -1.0, None, ALU.mult).then_inc(s_v0, 1)

            def conv(g, grp):
                dve.wait_ge(s_cv, g * 8 + 4 * grp + 4)
                for sh in range(1, 4):
                    for n in range(4):
                        tile = grp * 4 + n
                        m = stt(out=pend[:, tile, sh:T], in0=pg[grp][:, n * T:(n + 1) * T - sh],
                                scalar=cwc[:, 3 - sh, tile:tile + 1], in1=pend[:, tile, sh:T],
                                op0=ALU.mult, op1=ALU.add)
                        if sh < 3 and n == 3:
                            link(m)
                m.then_inc(s_cd, 1)

            def bc_heads(m):
                return m[:].unsqueeze(1).broadcast_to([P, 8, P])

            def delta(it, mods):
                bp, ba, bv = it * len(PEO), it * len(AO), it * len(VO)
                def PEw(name): dve.wait_ge(s_pe, bp + PEO[name])
                def Ac(name): dve.wait_ge(s_a, ba + AO0 + AO[name])
                def done(m): m.then_inc(s_v, 1)
                restart()
                dve.wait_ge(s_v0, V0["tok"])
                link(v.tensor_copy(tkc, tk[:, :, bass.ds(it * VH, VH)]))
                if mods:
                    done(taps(it + 1))
                else:
                    dve.sem_inc(s_v, 1)
                Ac("rn")
                done(v.tensor_tensor(qk.rearrange("p a b -> p (a b)"), qk.rearrange("p a b -> p (a b)"), rnb, ALU.mult))
                PEw("rows")
                for c in range(TT):
                    for h in range(VH):
                        n = c * VH + h
                        m = stt(out=dTb[:, n, :], in0=pd[1][:, n * P:(n + 1) * P], scalar=tkc[:, c, h:h + 1], in1=mneg[:],
                                op0=ALU.subtract, op1=ALU.min)
                done(m)
                yield
                PEw("gram")
                Ac("exp")
                for c in range(TT):
                    for h in range(VH):
                        n, b = c * VH + h, c * 2 + h // 2
                        m = stt(out=lTb[:, n, :], in0=pd[0][:, b * P:(b + 1) * P], scalar=tkc[:, 2 + c, h:h + 1],
                                in1=dTb[:, n, :], op0=ALU.mult, op1=ALU.mult)
                done(m)
                for b in range(4):
                    m = v.tensor_tensor(aTb[:, 2 * b:2 * b + 2, :],
                                        pd[0][:, 512 + b * P:512 + (b + 1) * P].unsqueeze(1).broadcast_to([P, 2, P]),
                                        dTb[:, 2 * b:2 * b + 2, :], ALU.mult)
                done(m)
                dve.wait_ge(s_v, bv + VO["lt"])
                link(v.tensor_tensor(Ub, lTb, bc_heads(m1t), ALU.mult))
                done(v.tensor_tensor(Ub, bc_heads(ident), Ub, ALU.subtract))
                yield
                par = 0
                Xf, Tf, Uf = (b.rearrange("p a b -> p (a b)") for b in (Xb, Tb, Ub))
                for s in LEVELS:
                    PEw(f"x{s}")
                    done(v.tensor_tensor(Xb, pd[par][:].rearrange("p (a b) -> p a b", b=P), bc_heads(msk[s]), ALU.mult))
                    par ^= 1
                    yield
                    PEw(f"tx{s}")
                    done(v.tensor_tensor(Tf, Tf, pd[par][:], ALU.subtract))
                    if s == 2:
                        pass
                    par ^= 1
                    par ^= 1
                    yield
                PEw("x64")
                done(v.tensor_tensor(Xb, pd[par][:].rearrange("p (a b) -> p a b", b=P), bc_heads(msk[64]), ALU.mult))
                yield
                PEw("ux64")
                done(v.tensor_tensor(Uf, Uf, pd[0][:], ALU.subtract))
                yield
                PEw("o0")
                done(v.tensor_copy(ob[:, 0:VH, :].rearrange("p a b -> p (a b)"), pd[0][:, 512:1024]))
                yield
                PEw("r")
                for h in range(VH):
                    m = stt(out=rhs1[:, h, :], in0=pd[1][:, h * P:(h + 1) * P], scalar=tkc[:, 5, h:h + 1],
                            in1=vtok[:, VH + h, :], op0=ALU.mult, op1=ALU.add)
                done(m)
                yield
                PEw("o1")
                done(v.tensor_tensor(ob[:, VH:8, :].rearrange("p a b -> p (a b)"),
                                     ob[:, VH:8, :].rearrange("p a b -> p (a b)"), pd[1][:, 0:512], ALU.add))
                Ac("rstd")
                done(v.tensor_tensor(ob, ob, rstd.unsqueeze(2).broadcast_to([P, 8, P]), ALU.mult))
                yield

            def finish(it):
                def PEw(name): dve.wait_ge(s_pe, it * len(PEO) + PEO[name])
                PEw("otr")
                dve.wait_ge(s_a, it * len(AO) + AO0)
                for c in range(TT):
                    m = stt(out=oT[:, bass.ds(it * VH, VH), c * P:(c + 1) * P],
                            in0=pd[0][:, c * 512:(c + 1) * 512].rearrange("p (h t) -> p h t", h=VH),
                            scalar=vc[:, V_NW:V_NW + 1], in1=zT[:, :, c * P:(c + 1) * P], op0=ALU.mult, op1=ALU.mult)
                m.then_inc(s_v, 1)
                PEw("mod")
                v.tensor_tensor(modt[:, bass.ds(it * 8 + 32, 8)], pd[1][:, 0:8],
                                vc[:, bass.ds(it * 8 + V_MODB + 32, 8)], ALU.add).then_inc(s_v, 1)

            for grp in range(2):
                conv(0, grp)
            with dve.Fori(0, NIT - 1) as j:
                steps = delta(j, True)
                for t in range(18):
                    next(steps, None)
                    if t == 5:
                        conv(j + 1, 0)
                    if t == 13:
                        conv(j + 1, 1)
                    if t % 2 and t < 16:
                        mod_units(j * 8 + 32, t // 2, 1)
                finish(j)
            fl = lambda x: x.rearrange("p a b -> p (a b)")

            def low(j, per, c):
                dve.wait_ge(s_hc, j * per + (c + 1))
                v.tensor_tensor(wl[c % 4][:], wraw[c % 4], wh[c % 4][:].bitcast(F32), ALU.subtract).then_inc(s_lc, 1)

            def stream(j, per, c, n, events={}):
                for t in range(n):
                    if not (isinstance(j, int) and c + t + AHEAD >= CK_END):
                        low(j, per, c + t + AHEAD)
                    if t in events:
                        events[t]()

            def used(j, per, c):
                dve.wait_ge(s_ck, j * per + (c + 5))

            dve.sem_inc(s_lc, 4)
            steps = delta(NIT - 1, False)
            for t in range(18):
                next(steps, None)
                if t % 2 and t < 16:
                    mod_units(NIT * 8 + 24, t // 2, 1)
            finish(NIT - 1)
            for c in range(AHEAD):
                low(0, 0, c)

            def o_low(i):
                dve.wait_ge(s_oh, i + 1)
                c = O_ORDER[i]
                k = slice(4 * c, 4 * c + 4)
                v.tensor_tensor(fl(o_s[1][:, k, :]), fl(oT[:, k, :]), fl(o_s[0][:, k, :]).bitcast(F32), ALU.subtract)\
                    .then_inc(s_os, 1)
            o_low(0)
            o_low(1)

            def factors():
                restart()
                lng, lnb = vc[:, V_LNG:V_LNG + KD], vc[:, V_LNB:V_LNB + KD]
                link(v.tensor_scalar(ga1p, modt[:, 2 * KD:3 * KD], 1.0, None, ALU.add))
                link(v.tensor_scalar(sc2p, modt[:, 4 * KD:5 * KD], 1.0, None, ALU.add))
                link(v.tensor_tensor(g1, lng, sc2p, ALU.mult))
                link(v.tensor_tensor(b1, lnb, sc2p, ALU.mult))
                link(v.tensor_tensor(b1, b1, modt[:, 3 * KD:4 * KD], ALU.add))
                link(v.tensor_scalar(ag, lng, ALPHA, None, ALU.mult))
                link(v.tensor_scalar(ab, lnb, ALPHA, None, ALU.mult))
                link(v.tensor_scalar(ga2p, modt[:, 5 * KD:6 * KD], 1.0, None, ALU.add))
                link(v.tensor_scalar(xT[:], xT[:], ALPHA, None, ALU.mult))
                restart()

            def residual(g, bank, fac, sem):
                for n in range(4):
                    k = 4 * g + n
                    m = stt(out=xT[:, k, :], in0=bank[:, n * T:(n + 1) * T], scalar=fac[:, k:k + 1],
                            in1=xT[:, k, :], op0=ALU.mult, op1=ALU.add)
                m.then_inc(sem, 1)

            def centre(bank, n):
                dve.wait_ge(s_pn, n)
                for c in range(4):
                    v.tensor_tensor(xT[:, 4 * c:4 * c + 4, :], xT[:, 4 * c:4 * c + 4, :],
                                    bank[:, 0:T].unsqueeze(1).broadcast_to([P, 4, T]), ALU.subtract).then_inc(s_vn, 1)

            def parts(dst, k, src):
                link(v.tensor_copy(fl(dst[0][:, k, :]), fl(src)))
                return v.tensor_tensor(fl(dst[1][:, k, :]), fl(src), fl(dst[0][:, k, :]).bitcast(F32), ALU.subtract)

            def norm_out(first, tile):
                restart()
                for c in range(4):
                    tmp = (sg, hgt)[c % 2]
                    if c >= 2:
                        dve.wait_ge(s_vn, first + c - 2)
                    for n in range(4):
                        m = tile(4 * c + n, tmp[:, n, :])
                    link(m)
                    parts(h_s, slice(4 * c, 4 * c + 4), tmp).then_inc(s_vn, 1)

            ts, tt = v.tensor_scalar, v.tensor_tensor
            are, aim, ldt, dt, xr, th, r, phi, sn, sh, tA, tB, tC, tD, cs, den = (prm[:, i, :] for i in range(16))
            tint = prm[:, 16, :].bitcast(mybir.dt.int32)

            def mul(o, x, y): link(tt(o, x, y, ALU.mult))

            def log_steps():
                dve.wait_ge(s_raw, 16 * N_RAW)
                v.tensor_copy(araw[0:PAIRS, 2, :].rearrange("p (g q) -> p g q", g=2),
                              ldraw[0:PAIRS, :].unsqueeze(2).broadcast_to([PAIRS, 2, 64])).then_inc(s_vx, 1)

            def exp(o, x):
                yield link(ts(tA, x, -104.0, 89.0, ALU.max, ALU.min))
                yield link(ts(tB, tA, 1.0 / math.log(2.0), MAGIC, ALU.mult, ALU.add))
                yield link(ts(tB, tB, MAGIC, None, ALU.subtract))
                yield link(stt(out=tA, in0=tB, scalar=-LN2_HI, in1=tA, op0=ALU.mult, op1=ALU.add))
                yield link(stt(out=tA, in0=tB, scalar=-LN2_LO, in1=tA, op0=ALU.mult, op1=ALU.add))
                yield link(ts(tC, tA, 1.0 / math.factorial(8), None, ALU.mult))
                for n in range(7, 0, -1):
                    yield link(stt(out=tC, in0=tC, scalar=1.0 / math.factorial(n), in1=tA, op0=ALU.add, op1=ALU.mult))
                yield link(ts(tB, tB, 127.0, 0.0, ALU.add, ALU.max))
                yield link(ts(tint, tB, 8388608.0, None, ALU.mult))
                yield link(stt(out=o, in0=tC, scalar=1.0, in1=prm[:, 16, :], op0=ALU.add, op1=ALU.mult))

            def angles():
                dve.wait_ge(s_ap, 1)
                yield from exp(dt, ldt)
                yield mul(xr, are, dt)
                yield mul(th, aim, dt)
                yield from exp(rdec, xr)
                yield link(ts(tB, th, 1.0 / (2 * math.pi), MAGIC, ALU.mult, ALU.add))
                yield link(ts(tB, tB, MAGIC, None, ALU.subtract))
                yield link(stt(out=th, in0=tB, scalar=-TURN[0], in1=th, op0=ALU.mult, op1=ALU.add))
                yield link(stt(out=th, in0=tB, scalar=-TURN[1], in1=th, op0=ALU.mult, op1=ALU.add))
                yield link(stt(out=th, in0=tB, scalar=-TURN[2], in1=th, op0=ALU.mult, op1=ALU.add))
                ts(phi, th, 3.1415925, -3.1415925, ALU.min, ALU.max).then_inc(s_vx, 1)

            def inputs():
                dve.wait_ge(s_ap, 4)
                yield link(stt(out=tD, in0=sh, scalar=-2.0, in1=sh, op0=ALU.mult, op1=ALU.mult))
                yield link(ts(cs, tD, 1.0, None, ALU.add))
                yield link(stt(out=tA, in0=rdec, scalar=-1.0, in1=cs, op0=ALU.add, op1=ALU.mult))
                yield link(tt(tA, tA, tD, ALU.add))
                yield mul(tB, rdec, sn)
                yield mul(den, are, are)
                yield mul(tC, aim, aim)
                yield link(tt(den, den, tC, ALU.add))
                yield link(v.reciprocal(den, den))
                yield mul(tC, tA, are)
                yield mul(tD, tB, aim)
                yield link(tt(tC, tC, tD, ALU.add))
                yield mul(xr, tC, den)
                yield mul(tC, tB, are)
                yield mul(tD, tA, aim)
                yield link(tt(tC, tC, tD, ALU.subtract))
                yield mul(r, tC, den)
                wide = lambda x: x.unsqueeze(2).broadcast_to([P, PAIRS, 32])
                yield mul(bbar[0], braw[0], wide(xr))
                yield mul(btmp, braw[1], wide(r))
                yield link(tt(bbar[0], bbar[0], btmp, ALU.subtract))
                yield mul(bbar[1], braw[1], wide(xr))
                yield mul(btmp, braw[0], wide(r))
                tt(bbar[1], bbar[1], btmp, ALU.add).then_inc(s_vp, 1)

            def powers():
                for er, ei in ((E1r, E1i), (E16r, E16i)):
                    yield link(v.memset(er[:, :, 0:1], 1.0))
                    yield link(v.memset(ei[:, :, 0:1], 0.0))
                    n = 1
                    while n < 16:
                        w = lambda x: x.unsqueeze(2).broadcast_to([P, PAIRS, n])
                        t0, t1 = (btmp[:, :, 8 * i:8 * i + n] for i in range(2))
                        yield mul(t0, er[:, :, 0:n], w(cs))
                        yield mul(t1, ei[:, :, 0:n], w(sn))
                        yield link(tt(er[:, :, n:2 * n], t0, t1, ALU.subtract))
                        yield mul(t0, er[:, :, 0:n], w(sn))
                        yield mul(t1, ei[:, :, 0:n], w(cs))
                        yield link(tt(ei[:, :, n:2 * n], t0, t1, ALU.add))
                        yield mul(tA, sn, sn)
                        yield mul(tB, cs, sn)
                        yield mul(cs, cs, cs)
                        yield link(tt(cs, cs, tA, ALU.subtract))
                        yield link(ts(sn, tB, 2.0, None, ALU.mult))
                        n *= 2
                dve.sem_inc(s_vp, 1)

            def advance(gen, n):
                for _ in range(n):
                    next(gen, None)

            angle_steps, input_steps, power_steps = angles(), inputs(), powers()

            def beside(t):
                if t == 3:
                    factors()
                if t < 12 and t % 2 == 0:
                    o_low(t // 2 + 2)
                elif t == 13:
                    log_steps()
                elif 16 <= t < 24:
                    advance(angle_steps, 7)
                elif t == 24:
                    advance(angle_steps, 1000)
                elif 25 <= t < 37:
                    advance(input_steps, 4)
                elif t == 37:
                    advance(input_steps, 1000)
                g, _, last = out_chunk(t)
                if last:
                    used(0, 0, t)
                    residual(g, pg[g % 2], ga1p, s_ev)
            stream(0, 0, 0, CK_FF, {t: (lambda t=t: beside(t)) for t in range(CK_FF)})
            centre(pd[0], 1)
            dve.wait_ge(s_an, AN["rsa"])
            dve.wait_ge(s_vn, VN["da"] + 3)
            for c in range(4):
                t4 = xT[:, 4 * c:4 * c + 4, :]
                link(v.tensor_tensor(t4, t4, rs.unsqueeze(1).broadcast_to([P, 4, T]), ALU.mult))
            norm_out(VN["ha"], lambda k, o: v.tensor_scalar(o, xT[:, k, :], g1[:, k:k + 1], b1[:, k:k + 1],
                                                            ALU.mult, ALU.add))

            def hidden(j, per, c, it):
                restart()
                used(j, per, c)
                dve.wait_ge(s_sg, it + 1)
                v.tensor_tensor(fl(hgt), fl(sg), pg[1][:], ALU.mult).then_inc(s_hm, 1)
                dve.wait_ge(s_hm, it + 1)
                parts(hg_s, slice(0, 4), hgt).then_inc(s_hg, 1)

            def down(j, per, c, n):
                used(j, per, c)
                residual(n, pd[n % 2], ga2p, s_dn)
            stream(0, 0, CK_FF, 16, {**{t: (lambda: advance(power_steps, 7)) for t in range(15)},
                                     15: lambda: (advance(power_steps, 1000), hidden(0, 0, CK_FF + 15, 0))})
            dve.sem_inc(s_dn, 2)
            dve.wait_ge(s_an, AN["x1"])
            with dve.Fori(0, KF // 4 - 1) as j:
                stream(j, 24, CK_FB, 24, {**{9 + 2 * n: (lambda n=n: down(j, 24, CK_FB + 9 + 2 * n, n))
                                             for n in range(4)}, 23: lambda: hidden(j, 24, CK_FB + 23, j + 1)})
            stream(0, 0, CK_FD, 8, {1 + 2 * n: (lambda n=n: down(0, 0, CK_FD + 1 + 2 * n, n)) for n in range(4)})
            centre(pg[0], 3)
            dve.wait_ge(s_an, AN["rsb"])
            dve.wait_ge(s_vn, VN["db"] + 3)
            for c in range(4):
                t4 = xT[:, 4 * c:4 * c + 4, :]
                v.tensor_tensor(t4, t4, rs.unsqueeze(1).broadcast_to([P, 4, T]), ALU.mult).then_inc(s_vn, 1)
            dve.wait_ge(s_an, AN["rsc"])
            norm_out(VN["hc"], lambda k, o: stt(out=o, in0=xT[:, k, :], scalar=vc[:, V_NG + k:V_NG + k + 1], in1=rs,
                                                op0=ALU.mult, op1=ALU.mult))

            with dve.Fori(0, 2) as j:
                stream(j, 16, CK_HYB, 16)

            def pair(j, q):
                dve.wait_ge(s_h, j * 8 + (q + 2))
                dve.wait_ge(s_xp, j * 8 + (q + 1))
                dve.wait_ge(s_tab, j * 8 + (q + 2))
                c, sn = (tabs[q % 2][:, i, :].unsqueeze(1).broadcast_to([P, 2, T]) for i in range(2))
                x = pd[0][:, (q % 2) * 512:(q % 2 + 1) * 512].rearrange("p (a b) -> p a b", a=2)
                tt = v.tensor_tensor
                tt(p1, x, c, ALU.mult)
                link(tt(p2, x, sn, ALU.mult))
                tt(p1[:, 0, :], p1[:, 0, :], p2[:, 1, :], ALU.add)
                link(tt(p1[:, 1, :], p1[:, 1, :], p2[:, 0, :], ALU.subtract))
                dec = rdec[:, bass.ds(j * 8 + q, 1)].broadcast_to([P, T])
                for i in range(2):
                    m = v.tensor_tensor_scan(gst[:, i, :], dec, p1[:, i, :], 0.0, ALU.mult, ALU.add)
                link(m)
                tt(p1, gst, c, ALU.mult)
                link(tt(p2, gst, sn, ALU.mult))
                dve.wait_ge(s_yp, j * 8 + (q + 7))
                h = hst[q % 2]
                tt(h[:, 0, :], p1[:, 0, :], p2[:, 1, :], ALU.subtract)
                tt(h[:, 1, :], p1[:, 1, :], p2[:, 0, :], ALU.add).then_inc(s_h, 1)

            def tile_out(j, i):
                dve.wait_ge(s_yp, j * 8 + (12 + 4 * i))
                t = bass.ds(j * 2 + i, 1)
                stt(out=yb[:, t, :].squeeze(1), in0=ucur[i], scalar=vc[:, bass.ds(j * 2 + (V_DSK + i), 1)],
                    in1=pd[1][:, i * 512:i * 512 + T], op0=ALU.mult, op1=ALU.add).then_inc(s_yt, 1)

            dve.sem_inc(s_h, 2)
            dve.sem_inc(s_yt, 2)
            for sem in (s_bg, s_ya, s_m, s_ms):
                dve.sem_inc(sem, 1)

            def out_cg(j):
                used(j, 32, CK_MIX + 15)
                dve.wait_ge(s_cg, j + 1)
                v.tensor_tensor(fl(cgb), fl(cgb), pg[1][:], ALU.mult).then_inc(s_vo, 1)

            def taps(j):
                dve.wait_ge(s_tp, j + 1)
                for sh in (1, 2):
                    for n in range(4):
                        m = stt(out=cvb[:, n, sh:T], in0=cgb[:, n, 0:T - sh],
                                scalar=vc[:, bass.ds(j * 4 + (V_CW2 + (2 - sh) * KD + n), 1)], in1=cvb[:, n, sh:T],
                                op0=ALU.mult, op1=ALU.add)
                    link(m)

            def out_bg(j):
                used(j, 32, CK_MIX + 23)
                v.tensor_tensor(fl(cvb), fl(cvb), pg[0][:], ALU.mult).then_inc(s_bg, 1)

            def out_ya(j):
                dve.wait_ge(s_za, j + 2)
                dve.wait_ge(s_bg, j + 2)
                v.tensor_tensor(fl(yaT[:, bass.ds(j * 4, 4), :]), fl(cvb), fl(szb), ALU.mult).then_inc(s_ya, 1)
            with dve.Fori(0, 4) as j:
                restart()
                stream(j, 32, CK_MIX, 32, {
                    **{4 * q + 1: (lambda q=q: pair(j, q)) for q in range(8)},
                    15: lambda: out_cg(j), 18: lambda: taps(j), 19: lambda: tile_out(j, 0), 24: lambda: out_bg(j),
                    31: lambda: (out_ya(j), tile_out(j, 1))})

            def gelu_parts():
                restart()
                dve.wait_ge(s_gel, 1)
                parts(yb_s, slice(0, 8), yb).then_inc(s_yl, 1)

            def gated(i):
                k = slice(4 * i, 4 * i + 4)
                dve.wait_ge(s_glu, i + 1)
                link(v.tensor_tensor(fl(glu[:, k, :]), fl(glu[:, k, :]), fl(yb[:, k, :]), ALU.mult))
                link(v.tensor_tensor(fl(glu[:, k, :]), fl(glu[:, k, :]), fl(zb[:, k, :]), ALU.mult))
                parts(yg_s, k, glu[:, k, :]).then_inc(s_yg, 1)

            def ya_low(c):
                dve.wait_ge(s_yah, c + 1)
                k = slice(4 * c, 4 * c + 4)
                v.tensor_tensor(fl(ya_s[1][:, k, :]), fl(yaT[:, k, :]), fl(ya_s[0][:, k, :]).bitcast(F32), ALU.subtract)\
                    .then_inc(s_yal, 1)

            def out_a(j, per, c, n):
                used(j, per, c)
                dve.wait_ge(s_gate, n + 1)
                dve.wait_ge(s_ms, n + 1)
                v.tensor_tensor(fl(mt), fl(gat), pd[0][:], ALU.mult).then_inc(s_m, 1)

            def out_b(j, per, c, n):
                restart()
                used(j, per, c)
                dve.wait_ge(s_gb, n + 2)
                dve.wait_ge(s_m, n + 2)
                link(v.tensor_tensor(fl(gbt), fl(gbt), pg[1][:], ALU.mult))
                link(v.tensor_tensor(fl(mt), fl(mt), fl(gbt), ALU.add))
                parts(m_s, bass.ds(n * 4, 4), mt).then_inc(s_ms, 1)
            stream(0, 0, CK_GA, 8, {1: gelu_parts})
            stream(0, 0, CK_GLU, 8, {4: lambda: gated(0), 7: lambda: gated(1)})

            def tail(j, per, c, n, count, more={}):
                stream(j, per, c, count, {15: lambda: out_a(j, per, c + 15, n), 19: lambda: out_b(j, per, c + 19, n),
                                          **more})
            tail(0, 0, CK_TAIL, 0, 28, {t: (lambda t=t: ya_low(t)) for t in range(4)})
            with dve.Fori(1, 3) as j:
                tail(j, 28, CK_TAIL, j, 28)
            tail(0, 0, CK_LAST, 3, 20)

            def out_o(g):
                used(0, 0, CK_O + 8 * g + 7)
                k = slice(4 * g, 4 * g + 4)
                v.tensor_tensor(fl(xT[:, k, :]), fl(xT[:, k, :]), pd[g % 2][:], ALU.add).then_inc(s_x3, 1)
            stream(0, 0, CK_O, 32, {8 * g + 7: (lambda g=g: out_o(g)) for g in range(4)})
            dve.wait_ge(s_x3, 4)
            dve.wait_ge(s_an, AN["rsd"])
            for k in range(KD):
                m = stt(out=xo[:, k, :], in0=xT[:, k, :], scalar=vc[:, V_FG + k:V_FG + k + 1], in1=rs,
                        op0=ALU.mult, op1=ALU.mult)
                if k % 4 == 3:
                    m.then_inc(s_vn, 1)


_INS = ["x", "c", "mod_w", "mod_b", "ln_g", "ln_b", "ffn_w_gu", "ffn_w_down", "gdn_w_in", "gdn_conv_w", "gdn_a_log",
        "gdn_dt_bias", "gdn_norm_w", "gdn_w_out", "norm_g_2", "w_in_2", "conv_w_2", "w_out_a_2", "a_re_2", "a_im_2",
        "log_dt_2", "b_re_2", "b_im_2", "c_re_2", "c_im_2", "d_skip_2", "w_glu_2", "b_glu_2", "w_out_b_2", "w_o_2",
        "final_g_2"]


def kernel(**inputs):
    import numpy as np
    import concourse.bacc as bacc
    from concourse.bass_utils import run_bass_kernel_spmd

    nc = bacc.Bacc("TRN2", target_bir_lowering=False, num_devices=1)
    arrays, views = {}, {}
    for name in _INS:
        a = np.ascontiguousarray(inputs[name])
        arrays[f"in_{name}"] = a
        views[name] = nc.dram_tensor(f"in_{name}", a.shape, mybir.dt.from_np(a.dtype), kind="ExternalInput").ap()
    out = nc.dram_tensor("out", (1, T, D), F32, kind="ExternalOutput").ap()
    build(nc, views, out)
    r = run_bass_kernel_spmd(nc, [arrays], core_ids=[0])
    return r.results[0]["out"]
```
